# Optimizing a Trainium2 kernel written in Bass

```python
import math
import jax, jax.numpy as jnp
from jax import lax
import numpy as np

D_MODEL = 1024
BATCH = 1
SEQ = 512
DEPTH = 2

ATT_HEADS = 8
ATT_KV_HEADS = 2
HEAD_DIM = 64
IDX_HEADS = 8
IDX_DIM = 64
TOPK_MAX = 256
Q_BLOCK = 128
ROPE_THETA = 10000.0
RWKV_HEADS = 4
RWKV_HEAD = 64
RWKV_DECAY_LORA = 32
RWKV_A_LORA = 32
RWKV_MV_LORA = 32
RWKV_GATE_LORA = 64
RWKV_GN_EPS = 64e-5
GDN_HEADS = 4
GDN_HEAD = 64
GDN_CONV = 4
GDN_CHUNK = 64
D_FF = 2816
NORM_EPS = 1e-6

ATT_W = ATT_HEADS * HEAD_DIM
KV_W = ATT_KV_HEADS * HEAD_DIM
RWKV_W = RWKV_HEADS * RWKV_HEAD
GDN_W = GDN_HEADS * GDN_HEAD
MIX_W = ATT_W + RWKV_W + GDN_W
ATT_SPLITS = (ATT_W, KV_W, KV_W, IDX_HEADS * IDX_DIM, IDX_DIM, IDX_HEADS)
RWKV_SPLITS = (RWKV_W, RWKV_W, RWKV_W, RWKV_DECAY_LORA, RWKV_A_LORA, RWKV_GATE_LORA)
GDN_SPLITS = (GDN_W, GDN_W, GDN_W, GDN_W, GDN_HEADS, GDN_HEADS)
RWKV_IN = sum(RWKV_SPLITS)
GROUP_SPLITS = (sum(ATT_SPLITS), RWKV_IN, sum(GDN_SPLITS))
IN_W = sum(GROUP_SPLITS)


def split_cols(p, sizes):
    offs = [int(o) for o in np.cumsum(sizes)[:-1]]
    return jnp.split(p, offs, axis=-1)

def rms_norm(x, g, eps=NORM_EPS):
    xf = x.astype(jnp.float32)
    y = xf * lax.rsqrt(jnp.mean(xf * xf, axis=-1, keepdims=True) + eps)
    return (y * g.astype(jnp.float32)).astype(x.dtype)

def l2_normalize(x, eps):
    xf = x.astype(jnp.float32)
    return xf * lax.rsqrt(jnp.sum(xf * xf, axis=-1, keepdims=True) + eps)

def rope(x, pos):
    half = x.shape[-1] // 2
    inv = ROPE_THETA ** (-jnp.arange(half, dtype=jnp.float32) / half)
    ang = pos.astype(jnp.float32)[:, None] * inv[None, :]
    cos, sin = jnp.cos(ang)[:, None, :], jnp.sin(ang)[:, None, :]
    xf = x.astype(jnp.float32)
    x1, x2 = xf[..., :half], xf[..., half:]
    return jnp.concatenate([x1 * cos - x2 * sin, x2 * cos + x1 * sin], axis=-1).astype(x.dtype)

def swiglu(h, w_gate, w_up, w_down):
    return (jax.nn.silu(h @ w_gate) * (h @ w_up)) @ w_down

def dsa_attention(pa, q_norm, k_norm):
    B, L, _ = pa.shape
    q, k, v, qi, ki, wi = split_cols(pa, ATT_SPLITS)
    pos = jnp.arange(L)
    q = rope(rms_norm(q.reshape(B, L, ATT_HEADS, HEAD_DIM), q_norm), pos)
    k = rope(rms_norm(k.reshape(B, L, ATT_KV_HEADS, HEAD_DIM), k_norm), pos)
    v = v.reshape(B, L, ATT_KV_HEADS, HEAD_DIM)
    qi = rope(qi.reshape(B, L, IDX_HEADS, IDX_DIM), pos).astype(jnp.float32)
    ki = rope(ki[:, :, None, :], pos)[:, :, 0].astype(jnp.float32)
    wi = wi.astype(jnp.float32) * (IDX_HEADS ** -0.5 * IDX_DIM ** -0.5)
    n_sel = min(TOPK_MAX, L // 4)
    n_blk = L // Q_BLOCK
    rep = ATT_HEADS // ATT_KV_HEADS
    scale = HEAD_DIM ** -0.5

    def to_blocks(a):
        return a.reshape(B, n_blk, Q_BLOCK, *a.shape[2:]).swapaxes(0, 1)

    def block(args):
        qb, qib, wib, tb = args
        logits = jnp.einsum('bqhd,bsd->bqhs', qib, ki)
        score = jnp.einsum('bqhs,bqh->bqs', jax.nn.relu(logits), wib)
        score = jnp.where(pos[None, None, :] <= tb[None, :, None], score, -jnp.inf)
        _, idx = lax.top_k(score, n_sel)
        valid = idx <= tb[None, :, None]
        ks = jax.vmap(lambda kb, ib: kb[ib])(k, idx).astype(jnp.float32)
        vs = jax.vmap(lambda vb, ib: vb[ib])(v, idx)
        qg = qb.reshape(B, Q_BLOCK, ATT_KV_HEADS, rep, HEAD_DIM).astype(jnp.float32)
        s = jnp.einsum('bqgrd,bqkgd->bqgrk', qg, ks) * scale
        s = jnp.where(valid[:, :, None, None, :], s, -jnp.inf)
        p = jax.nn.softmax(s, axis=-1).astype(vs.dtype)
        o = jnp.einsum('bqgrk,bqkgd->bqgrd', p, vs)
        return o.reshape(B, Q_BLOCK, ATT_W)

    out = lax.map(block, (to_blocks(q), to_blocks(qi), to_blocks(wi), pos.reshape(n_blk, Q_BLOCK)))
    return out.swapaxes(0, 1).reshape(B, L, ATT_W).astype(pa.dtype)

def rwkv7_scan(r, w, k, v, a, b):
    B, L, H, N = r.shape

    def step(S, inp):
        rt, wt, kt, vt, at, bt = inp
        sa = jnp.einsum('bhij,bhj->bhi', S, at)
        S = S * wt[:, :, None, :] + sa[..., None] * bt[:, :, None, :] + vt[..., None] * kt[:, :, None, :]
        return S, jnp.einsum('bhij,bhj->bhi', S, rt)

    xs = tuple(jnp.moveaxis(t, 1, 0) for t in (r, w, k, v, a, b))
    _, y = lax.scan(step, jnp.zeros((B, H, N, N), jnp.float32), xs)
    return jnp.moveaxis(y, 0, 1)

def rwkv7_time_mix(pb, mu, w0, w_up, a0, a_up, g_up, k_k, k_a, r_k, gn_w, gn_b, v_first, v0, v_down, v_up):
    dt = pb.dtype
    B, L, _ = pb.shape
    hb = pb.astype(jnp.float32)
    prev = jnp.pad(hb, ((0, 0), (1, 0), (0, 0)))[:, :-1]
    hb = hb + (prev - hb) * mu
    r, k, v, wd, ad, gd = split_cols(hb, RWKV_SPLITS)
    heads = lambda t: t.reshape(B, L, RWKV_HEADS, RWKV_HEAD)
    w_log = -jax.nn.softplus(-(w0 + jnp.tanh(wd) @ w_up)) - 0.5
    decay = jnp.exp(-jnp.exp(w_log))
    a = jax.nn.sigmoid(a0 + ad @ a_up)
    g = jax.nn.sigmoid(gd) @ g_up
    kk = l2_normalize(heads(k * k_k), 1e-12)
    k = k * (1.0 + (a - 1.0) * k_a)
    if v_first is None:
        v_first = v
    else:
        v = v + (v_first - v) * jax.nn.sigmoid(v0 + (v @ v_down) @ v_up)
    rh, kh, vh = heads(r), heads(k), heads(v)
    y = rwkv7_scan(rh, heads(decay), kh, vh, -kk, kk * heads(a))
    mean = jnp.mean(y, axis=-1, keepdims=True)
    var = jnp.mean(jnp.square(y - mean), axis=-1, keepdims=True)
    y = ((y - mean) * lax.rsqrt(var + RWKV_GN_EPS)).reshape(B, L, RWKV_W) * gn_w + gn_b
    bonus = jnp.sum(rh * kh * r_k, axis=-1, keepdims=True) * vh
    y = (y + bonus.reshape(B, L, RWKV_W)) * g
    return y.astype(dt), v_first

def causal_dwconv(x, w):
    C = x.shape[-1]
    return lax.conv_general_dilated(x, w[:, None, :], window_strides=(1,), padding=[(w.shape[0] - 1, 0)],
                                    dimension_numbers=('NWC', 'WIO', 'NWC'), feature_group_count=C)

def chunk_gated_delta_rule(q, k, v, g, beta):
    B, L, H, Dk = q.shape
    Dv = v.shape[-1]
    C = GDN_CHUNK
    n = L // C
    chunks = lambda t: t.reshape(B, n, C, H, t.shape[-1]).transpose(0, 3, 1, 2, 4)
    q, k, v = chunks(q), chunks(k), chunks(v)
    beta = beta.reshape(B, n, C, H).transpose(0, 3, 1, 2)
    g = jnp.cumsum(g.reshape(B, n, C, H).transpose(0, 3, 1, 2), axis=-1)
    incl = jnp.tril(jnp.ones((C, C), bool))
    strict = jnp.tril(jnp.ones((C, C), bool), -1)
    decay = jnp.exp(jnp.where(incl, g[..., :, None] - g[..., None, :], -jnp.inf))
    kb = k * beta[..., None]
    lower = jnp.where(strict, jnp.einsum('bhncd,bhnsd->bhncs', kb, k) * decay, 0.0)
    rhs = jnp.concatenate([v * beta[..., None], kb * jnp.exp(g)[..., None]], axis=-1)
    sol = lax.linalg.triangular_solve(jnp.eye(C, dtype=jnp.float32) + lower, rhs,
                                      left_side=True, lower=True, unit_diagonal=True)
    u, wk = sol[..., :Dv], sol[..., Dv:]
    intra = jnp.where(incl, jnp.einsum('bhncd,bhnsd->bhncs', q, k) * decay, 0.0)

    def step(S, inp):
        qc, kc, uc, wc, gc, ac = inp
        v_new = uc - jnp.einsum('bhck,bhkv->bhcv', wc, S)
        o = jnp.einsum('bhck,bhkv->bhcv', qc * jnp.exp(gc)[..., None], S) + jnp.einsum('bhcs,bhsv->bhcv', ac, v_new)
        g_last = gc[..., -1]
        S = S * jnp.exp(g_last)[..., None, None] + jnp.einsum(
            'bhck,bhcv->bhkv', kc * jnp.exp(g_last[..., None] - gc)[..., None], v_new)
        return S, o

    xs = tuple(jnp.moveaxis(t, 2, 0) for t in (q, k, u, wk, g, intra))
    _, o = lax.scan(step, jnp.zeros((B, H, Dk, Dv), jnp.float32), xs)
    return o.transpose(1, 0, 3, 2, 4).reshape(B, L, H, Dv)

def gated_deltanet(pc, conv_w, a_log, dt_bias, o_norm):
    dt = pc.dtype
    B, L, _ = pc.shape
    q, k, v, z, b_in, a_in = split_cols(pc.astype(jnp.float32), GDN_SPLITS)
    qkv = jax.nn.silu(causal_dwconv(jnp.concatenate([q, k, v], axis=-1), conv_w.astype(jnp.float32)))
    q, k, v = jnp.split(qkv, 3, axis=-1)
    heads = lambda t: t.reshape(B, L, GDN_HEADS, GDN_HEAD)
    q = l2_normalize(heads(q), 1e-6) * (GDN_HEAD ** -0.5)
    k = l2_normalize(heads(k), 1e-6)
    beta = jax.nn.sigmoid(b_in)
    g = -jnp.exp(a_log.astype(jnp.float32)) * jax.nn.softplus(a_in + dt_bias)
    o = chunk_gated_delta_rule(q, k, heads(v), g, beta)
    o = rms_norm(o, o_norm) * jax.nn.silu(heads(z))
    return o.reshape(B, L, GDN_W).astype(dt)

def first_inputs(seed: int = 0) -> dict:
    key = jax.random.key(seed)
    ks = iter(jax.random.split(key, 40))
    nrm = lambda shape, s: jax.random.normal(next(ks), shape, jnp.float32) * s
    uni = lambda shape, lo, hi: jax.random.uniform(next(ks), shape, jnp.float32, lo, hi)
    D, F = D_MODEL, D_FF
    dt0 = jnp.exp(uni((DEPTH, GDN_HEADS), math.log(1e-3), math.log(1e-1)))
    return {
        'x': nrm((BATCH, SEQ, D), 1.0),
        'ffn_norm': 1.0 + nrm((DEPTH, 2, D), 0.02),
        'ffn_w_gate': nrm((DEPTH, 2, D, F), D ** -0.5),
        'ffn_w_up': nrm((DEPTH, 2, D, F), D ** -0.5),
        'ffn_w_down': nrm((DEPTH, 2, F, D), F ** -0.5),
        'mix_norm': 1.0 + nrm((DEPTH, D), 0.02),
        'w_in': nrm((DEPTH, D, IN_W), D ** -0.5),
        'w_out': nrm((DEPTH, MIX_W, D), MIX_W ** -0.5),
        'att_q_norm': 1.0 + nrm((DEPTH, HEAD_DIM), 0.02),
        'att_k_norm': 1.0 + nrm((DEPTH, HEAD_DIM), 0.02),
        'rwkv_mu': uni((DEPTH, RWKV_IN), 0.0, 1.0),
        'rwkv_w0': uni((DEPTH, RWKV_W), -6.5, -1.5),
        'rwkv_w_up': nrm((DEPTH, RWKV_DECAY_LORA, RWKV_W), RWKV_DECAY_LORA ** -0.5),
        'rwkv_a0': nrm((DEPTH, RWKV_W), 0.1),
        'rwkv_a_up': nrm((DEPTH, RWKV_A_LORA, RWKV_W), RWKV_A_LORA ** -0.5),
        'rwkv_g_up': nrm((DEPTH, RWKV_GATE_LORA, RWKV_W), RWKV_GATE_LORA ** -0.5),
        'rwkv_k_k': 0.85 + nrm((DEPTH, RWKV_W), 0.05),
        'rwkv_k_a': 1.0 + nrm((DEPTH, RWKV_W), 0.05),
        'rwkv_r_k': nrm((DEPTH, RWKV_HEADS, RWKV_HEAD), 0.1),
        'rwkv_gn_w': 1.0 + nrm((DEPTH, RWKV_W), 0.02),
        'rwkv_gn_b': nrm((DEPTH, RWKV_W), 0.02),
        'rwkv_v0': 1.0 + nrm((DEPTH - 1, RWKV_W), 0.05),
        'rwkv_v_down': nrm((DEPTH - 1, RWKV_W, RWKV_MV_LORA), RWKV_W ** -0.5),
        'rwkv_v_up': nrm((DEPTH - 1, RWKV_MV_LORA, RWKV_W), 0.1 * RWKV_MV_LORA ** -0.5),
        'gdn_conv': nrm((DEPTH, GDN_CONV, 3 * GDN_W), GDN_CONV ** -0.5),
        'gdn_a_log': jnp.log(uni((DEPTH, GDN_HEADS), 1.0, 16.0)),
        'gdn_dt_bias': dt0 + jnp.log(-jnp.expm1(-dt0)),
        'gdn_o_norm': 1.0 + nrm((DEPTH, GDN_HEAD), 0.02),
    }

def first_block(x, ffn_norm, ffn_w_gate, ffn_w_up, ffn_w_down, mix_norm, w_in, w_out, att_q_norm, att_k_norm,
              rwkv_mu, rwkv_w0, rwkv_w_up, rwkv_a0, rwkv_a_up, rwkv_g_up, rwkv_k_k, rwkv_k_a, rwkv_r_k,
              rwkv_gn_w, rwkv_gn_b, rwkv_v0, rwkv_v_down, rwkv_v_up, gdn_conv, gdn_a_log, gdn_dt_bias, gdn_o_norm):
    v_first = None
    for l in range(DEPTH):
        x = x + 0.5 * swiglu(rms_norm(x, ffn_norm[l, 0]), ffn_w_gate[l, 0], ffn_w_up[l, 0], ffn_w_down[l, 0])
        p = rms_norm(x, mix_norm[l]) @ w_in[l]
        pa, pb, pc = split_cols(p, GROUP_SPLITS)
        ya = dsa_attention(pa, att_q_norm[l], att_k_norm[l])
        if l == 0:
            vres = (None, None, None)
        else:
            vres = (rwkv_v0[l - 1], rwkv_v_down[l - 1], rwkv_v_up[l - 1])
        yb, v_first = rwkv7_time_mix(pb, rwkv_mu[l], rwkv_w0[l], rwkv_w_up[l], rwkv_a0[l], rwkv_a_up[l],
                                     rwkv_g_up[l], rwkv_k_k[l], rwkv_k_a[l], rwkv_r_k[l], rwkv_gn_w[l],
                                     rwkv_gn_b[l], v_first, *vres)
        yc = gated_deltanet(pc, gdn_conv[l], gdn_a_log[l], gdn_dt_bias[l], gdn_o_norm[l])
        x = x + jnp.concatenate([ya, yb, yc], axis=-1) @ w_out[l]
        x = x + 0.5 * swiglu(rms_norm(x, ffn_norm[l, 1]), ffn_w_gate[l, 1], ffn_w_up[l, 1], ffn_w_down[l, 1])
    return x


GRID_W = 64
CTX_LEN = 256
N_EVEN = (DEPTH + 1) // 2
N_ODD = DEPTH // 2

MLA_HEADS = 8
QK_NOPE_DIM = 64
QK_ROPE_DIM = 32
QK_HEAD_DIM = QK_NOPE_DIM + QK_ROPE_DIM
V_HEAD_DIM = 64
Q_LORA_RANK = 384
KV_LORA_RANK = 256
QK_SCALE = QK_HEAD_DIM ** -0.5
ROPE_BASE = 10000.0
BLOCK_Q = 128
CONV_GROUPS = 8
CONV_GROUP_DIM = 64
CONV_DIM = CONV_GROUPS * CONV_GROUP_DIM
CONV_WIDTH = 3
CONV_OFFSET = Q_LORA_RANK + KV_LORA_RANK + QK_ROPE_DIM
IN_PROJ_DIM = CONV_OFFSET + 3 * CONV_DIM
MIX_OUT_DIM = MLA_HEADS * V_HEAD_DIM + CONV_DIM
FOURIER_GROUPS = 4
FOURIER_GROUP_DIM = D_MODEL // FOURIER_GROUPS
D_FF_2 = ((8 * D_MODEL + 3 * 256 - 1) // (3 * 256)) * 256
EPS = 1e-6


def rmsnorm(x, g):
    xf = x.astype(jnp.float32)
    y = xf * lax.rsqrt(jnp.mean(xf * xf, axis=-1, keepdims=True) + EPS)
    return (y * g.astype(jnp.float32)).astype(x.dtype)

def axial_angles(T):
    rows = T // GRID_W
    row = jnp.broadcast_to(jnp.arange(rows)[:, None], (rows, GRID_W)).reshape(-1).astype(jnp.float32)
    col = jnp.broadcast_to(jnp.arange(GRID_W)[None, :], (rows, GRID_W)).reshape(-1).astype(jnp.float32)
    half = QK_ROPE_DIM // 2
    inv = 1.0 / (ROPE_BASE ** (jnp.arange(0, half, 2, dtype=jnp.float32) / half))
    return row[:, None] * inv, col[:, None] * inv

def rotate(x, ang):
    cos = jnp.cos(ang)[:, None, :].astype(x.dtype)
    sin = jnp.sin(ang)[:, None, :].astype(x.dtype)
    x1, x2 = jnp.split(x, 2, axis=-1)
    return jnp.concatenate([x1 * cos - x2 * sin, x2 * cos + x1 * sin], axis=-1)

def axial_rope(x, ang_row, ang_col):
    half = QK_ROPE_DIM // 2
    return jnp.concatenate([rotate(x[..., :half], ang_row), rotate(x[..., half:], ang_col)], axis=-1)

def mla_qkv(proj, q_norm_g, kv_norm_g, w_uq, w_ukv, q_gain, k_gain, angles):
    B, T, _ = proj.shape
    cq = proj[..., :Q_LORA_RANK]
    ckv = proj[..., Q_LORA_RANK:Q_LORA_RANK + KV_LORA_RANK]
    k_pe = proj[..., Q_LORA_RANK + KV_LORA_RANK:CONV_OFFSET]
    q = (rmsnorm(cq, q_norm_g) @ w_uq).reshape(B, T, MLA_HEADS, QK_HEAD_DIM)
    kv = (rmsnorm(ckv, kv_norm_g) @ w_ukv).reshape(B, T, MLA_HEADS, QK_NOPE_DIM + V_HEAD_DIM)
    k_nope, v = kv[..., :QK_NOPE_DIM], kv[..., QK_NOPE_DIM:]
    k = jnp.concatenate([k_nope, jnp.broadcast_to(k_pe[:, :, None, :], (B, T, MLA_HEADS, QK_ROPE_DIM))], axis=-1)
    q = rmsnorm(q, q_gain)
    k = rmsnorm(k, k_gain)
    if angles is not None:
        ang_row, ang_col = angles
        q = jnp.concatenate([q[..., :QK_NOPE_DIM], axial_rope(q[..., QK_NOPE_DIM:], ang_row, ang_col)], axis=-1)
        k = jnp.concatenate([k[..., :QK_NOPE_DIM], axial_rope(k[..., QK_NOPE_DIM:], ang_row, ang_col)], axis=-1)
    return q, k, v

def attend(q, k, v):
    s = jnp.einsum('bqhd,bkhd->bhqk', q, k, preferred_element_type=jnp.float32) * QK_SCALE
    p = jax.nn.softmax(s, axis=-1)
    return jnp.einsum('bhqk,bkhd->bqhd', p.astype(v.dtype), v)

def attend_blocked(q, k, v):
    B, S, H, D = q.shape
    nb = S // BLOCK_Q
    qb = q.reshape(B, nb, BLOCK_Q, H, D).transpose(1, 0, 2, 3, 4)
    ob = lax.map(lambda qi: attend(qi, k, v), qb)
    return ob.transpose(1, 0, 2, 3, 4).reshape(B, S, H * V_HEAD_DIM)

def short_conv(p, conv_w):
    b_gate, c_gate, u = jnp.split(p, 3, axis=-1)
    z = c_gate * u
    T = z.shape[1]
    zp = jnp.pad(z, ((0, 0), (1, 1), (0, 0)))
    y = zp[:, 0:T] * conv_w[0] + zp[:, 1:T + 1] * conv_w[1] + zp[:, 2:T + 2] * conv_w[2]
    return b_gate * y

def even_mixer(h_lat, h_ctx, w_in, q_norm_g, kv_norm_g, w_uq, w_ukv, q_gain, k_gain, conv_w, w_o, with_ctx_out):
    B, S, _ = h_lat.shape
    L = h_ctx.shape[1]
    p_lat = h_lat @ w_in
    p_ctx = h_ctx @ w_in
    q_l, k_l, v_l = mla_qkv(p_lat, q_norm_g, kv_norm_g, w_uq, w_ukv, q_gain, k_gain, axial_angles(S))
    q_c, k_c, v_c = mla_qkv(p_ctx, q_norm_g, kv_norm_g, w_uq, w_ukv, q_gain, k_gain, None)
    k_all = jnp.concatenate([k_l, k_c], axis=1)
    v_all = jnp.concatenate([v_l, v_c], axis=1)
    a_l = attend_blocked(q_l, k_all, v_all)
    s_l = short_conv(p_lat[..., CONV_OFFSET:], conv_w)
    out_l = jnp.concatenate([a_l, s_l], axis=-1) @ w_o
    if not with_ctx_out:
        return out_l, None
    a_c = attend(q_c, k_c, v_c).reshape(B, L, MLA_HEADS * V_HEAD_DIM)
    s_c = short_conv(p_ctx[..., CONV_OFFSET:], conv_w)
    out_c = jnp.concatenate([a_c, s_c], axis=-1) @ w_o
    return out_l, out_c

def fourier_mixer(h, w_f):
    B, T, _ = h.shape
    hg = h.astype(jnp.float32).reshape(B, T, FOURIER_GROUPS, FOURIER_GROUP_DIM)
    f = jnp.fft.fft2(hg, axes=(1, 3), norm="ortho").real
    return f.reshape(B, T, D_MODEL).astype(h.dtype) @ w_f

def swiglu_2(h, w1, w3, w2):
    return (jax.nn.silu(h @ w1) * (h @ w3)) @ w2

def ada(cvec, w, b):
    return jnp.split(jax.nn.silu(cvec) @ w + b, 6, axis=-1)

def second_inputs(seed: int = 0) -> dict:
    key = jax.random.key(seed)
    ks = jax.random.split(key, 24)
    nrm = jax.random.normal
    f32 = jnp.float32
    D = D_MODEL
    return {
        "x": nrm(ks[0], (BATCH, SEQ, D), f32),
        "c": nrm(ks[1], (BATCH, D), f32),
        "ctx": nrm(ks[2], (BATCH, CTX_LEN, D), f32),
        "c_ctx": nrm(ks[3], (D,), f32),
        "ada_w": nrm(ks[4], (DEPTH, D, 6 * D), f32) * D ** -0.5,
        "ada_b": nrm(ks[5], (DEPTH, 6 * D), f32) * 0.01,
        "norm1_g": 1.0 + 0.02 * nrm(ks[6], (DEPTH, D), f32),
        "norm2_g": 1.0 + 0.02 * nrm(ks[7], (DEPTH, D), f32),
        "w_in": nrm(ks[8], (N_EVEN, D, IN_PROJ_DIM), f32) * D ** -0.5,
        "q_norm_g": 1.0 + 0.02 * nrm(ks[9], (N_EVEN, Q_LORA_RANK), f32),
        "kv_norm_g": 1.0 + 0.02 * nrm(ks[10], (N_EVEN, KV_LORA_RANK), f32),
        "w_uq": nrm(ks[11], (N_EVEN, Q_LORA_RANK, MLA_HEADS * QK_HEAD_DIM), f32) * Q_LORA_RANK ** -0.5,
        "w_ukv": nrm(ks[12], (N_EVEN, KV_LORA_RANK, MLA_HEADS * (QK_NOPE_DIM + V_HEAD_DIM)), f32) * KV_LORA_RANK ** -0.5,
        "q_gain": 1.0 + 0.02 * nrm(ks[13], (N_EVEN, QK_HEAD_DIM), f32),
        "k_gain": 1.0 + 0.02 * nrm(ks[14], (N_EVEN, QK_HEAD_DIM), f32),
        "conv_w": nrm(ks[15], (N_EVEN, CONV_WIDTH, CONV_DIM), f32) * CONV_WIDTH ** -0.5,
        "w_o": nrm(ks[16], (N_EVEN, MIX_OUT_DIM, D), f32) * MIX_OUT_DIM ** -0.5,
        "w_fourier": nrm(ks[17], (N_ODD, D, D), f32) * D ** -0.5,
        "ffn_w1": nrm(ks[18], (DEPTH, D, D_FF_2), f32) * D ** -0.5,
        "ffn_w3": nrm(ks[19], (DEPTH, D, D_FF_2), f32) * D ** -0.5,
        "ffn_w2": nrm(ks[20], (DEPTH, D_FF_2, D), f32) * D_FF_2 ** -0.5,
    }

def second_block(x, c, ctx, c_ctx, ada_w, ada_b, norm1_g, norm2_g, w_in, q_norm_g, kv_norm_g, w_uq, w_ukv,
              q_gain, k_gain, conv_w, w_o, w_fourier, ffn_w1, ffn_w3, ffn_w2):
    for i in range(DEPTH):
        last = i == DEPTH - 1
        j = i // 2
        sh1, sc1, g1, sh2, sc2, g2 = [m[:, None, :] for m in ada(c, ada_w[i], ada_b[i])]
        csh1, csc1, cg1, csh2, csc2, cg2 = ada(c_ctx, ada_w[i], ada_b[i])
        h_l = rmsnorm(x, norm1_g[i]) * (1 + sc1) + sh1
        if i % 2 == 0:
            h_c = rmsnorm(ctx, norm1_g[i]) * (1 + csc1) + csh1
            out_l, out_c = even_mixer(h_l, h_c, w_in[j], q_norm_g[j], kv_norm_g[j], w_uq[j], w_ukv[j],
                                      q_gain[j], k_gain[j], conv_w[j], w_o[j], not last)
        else:
            out_l = fourier_mixer(h_l, w_fourier[j])
            out_c = None
            if not last:
                h_c = rmsnorm(ctx, norm1_g[i]) * (1 + csc1) + csh1
                out_c = fourier_mixer(h_c, w_fourier[j])
        x = x + g1 * out_l
        x = x + g2 * swiglu_2(rmsnorm(x, norm2_g[i]) * (1 + sc2) + sh2, ffn_w1[i], ffn_w3[i], ffn_w2[i])
        if not last:
            ctx = ctx + cg1 * out_c
            ctx = ctx + cg2 * swiglu_2(rmsnorm(ctx, norm2_g[i]) * (1 + csc2) + csh2, ffn_w1[i], ffn_w3[i], ffn_w2[i])
    return x


def setup_inputs(seed=0):
    out = dict(first_inputs(seed))
    for name, value in second_inputs(seed + 1).items():
        if name != "x":
            out[name + "_2"] = value
    return out


def reference(
    x, ffn_norm, ffn_w_gate, ffn_w_up, ffn_w_down, mix_norm, w_in, w_out, att_q_norm,
    att_k_norm, rwkv_mu, rwkv_w0, rwkv_w_up, rwkv_a0, rwkv_a_up, rwkv_g_up, rwkv_k_k, rwkv_k_a,
    rwkv_r_k, rwkv_gn_w, rwkv_gn_b, rwkv_v0, rwkv_v_down, rwkv_v_up, gdn_conv, gdn_a_log,
    gdn_dt_bias, gdn_o_norm, c_2, ctx_2, c_ctx_2, ada_w_2, ada_b_2, norm1_g_2, norm2_g_2,
    w_in_2, q_norm_g_2, kv_norm_g_2, w_uq_2, w_ukv_2, q_gain_2, k_gain_2, conv_w_2, w_o_2,
    w_fourier_2, ffn_w1_2, ffn_w3_2, ffn_w2_2,
):
    x = first_block(
        x, ffn_norm, ffn_w_gate, ffn_w_up, ffn_w_down, mix_norm, w_in, w_out, att_q_norm,
        att_k_norm, rwkv_mu, rwkv_w0, rwkv_w_up, rwkv_a0, rwkv_a_up, rwkv_g_up, rwkv_k_k,
        rwkv_k_a, rwkv_r_k, rwkv_gn_w, rwkv_gn_b, rwkv_v0, rwkv_v_down, rwkv_v_up, gdn_conv,
        gdn_a_log, gdn_dt_bias, gdn_o_norm,
    )
    return second_block(
        x, c_2, ctx_2, c_ctx_2, ada_w_2, ada_b_2, norm1_g_2, norm2_g_2, w_in_2, q_norm_g_2,
        kv_norm_g_2, w_uq_2, w_ukv_2, q_gain_2, k_gain_2, conv_w_2, w_o_2, w_fourier_2,
        ffn_w1_2, ffn_w3_2, ffn_w2_2,
    )


_drawn_inputs = setup_inputs


def setup_inputs(seed=0):
    import zlib

    import numpy as np

    out = dict(_drawn_inputs(seed))
    spreads = {}
    factors = {'att_q_norm': 8.0,
     'att_k_norm': 8.0,
     'rwkv_a0': 3.08,
     'rwkv_gn_w': 5.625,
     'rwkv_gn_b': 5.206,
     'rwkv_v0': 8.0,
     'rwkv_v_down': 7.233,
     'rwkv_v_up': 7.099,
     'gdn_o_norm': 4.679,
     'ctx_2': 6.401,
     'ada_b_2': 2.751,
     'norm1_g_2': 2.783,
     'norm2_g_2': 4.311,
     'q_norm_g_2': 8.0,
     'kv_norm_g_2': 8.0,
     'q_gain_2': 8.0,
     'k_gain_2': 8.0}
    for name, (base, spread) in spreads.items():
        noise = np.random.default_rng([zlib.crc32(name.encode()), seed]).standard_normal(out[name].shape)
        drawn = base * np.exp(spread * noise) if base else spread * noise
        out[name] = __import__('jax').numpy.asarray(drawn.astype(out[name].dtype))
    for name, factor in factors.items():
        out[name] = (out[name] * factor).astype(out[name].dtype)
    return out
```

```python
from contextlib import ExitStack

import numpy as np

import concourse.bass as bass
from concourse import mybir

P = 128
T = 512
D = 1024
KD = D // P
FF = 2816
NF = FF // P
DEPTH = 2
TB = T // P
CTX = 256
TK = T + CTX
HD = 64
QKD = 96
NORM_EPS = 1e-6
RING = 4
FFN_ORDER = (7, 4, 5, 6, 0, 1, 2, 3)
TILE = 1024
LONE_PAIRS = NF // 2 % RING

F32 = mybir.dt.float32
F32R = mybir.dt.float32r
ALU = mybir.AluOpType
ACT = mybir.ActivationFunctionType
AX_X = mybir.AxisListType.X

ATT_TILES = 12
REC_TILES = 15
PHASES = []
for _layer in range(DEPTH):
    PHASES += [(f"ffn{2 * _layer}", 66), (f"att_in{_layer}", ATT_TILES), (f"rec_in{_layer}", REC_TILES),
               (f"mix_out{_layer}", KD), (f"ffn{2 * _layer + 1}", 66)]
PHASES += [("mla_in", 18), ("mla_q", 4), ("mla_kv", 3), ("mla_out", KD), ("ffn4", 66),
           ("dft_group", 1), ("dft_time", 4), ("fourier_out", KD), ("ffn5", 66)]
BASE = {}
N_TILES = 0
for _name, _n in PHASES:
    BASE[_name] = N_TILES
    N_TILES += _n
assert N_TILES % RING == 0
ADA_TILES = DEPTH * 6 * KD
ADA_PER_FFN = ADA_TILES // 4
ADA_CTX = 2 * KD

PARAMS = [("ffn_g", 6 * KD), ("mix_g", 4 * KD), ("ada_b", ADA_TILES)]
for _layer in range(DEPTH):
    PARAMS += [(f"mu{_layer}", 7)] + [(f"{n}{_layer}", 2) for n in ("w0", "a0", "k_k", "k_a", "r_k", "gn_w", "gn_b")]
    PARAMS += [(f"conv{_layer}", 24), (f"o_norm{_layer}", 1), (f"a_log{_layer}", 1), (f"dt{_layer}", 1)]
    PARAMS += [(f"att_q{_layer}", 1), (f"att_k{_layer}", 1)]
PARAMS += [("v0", 2), ("mla_qn", 3), ("mla_kvn", 2), ("q_gain", 1), ("k_gain", 1), ("short_conv", 12)]
PARAM_AT = {}
N_PARAMS = 0
for _name, _n in PARAMS:
    PARAM_AT[_name] = N_PARAMS
    N_PARAMS += _n

N_LEVELS = 7
CONSTS = [("ident", P), ("ones", P), ("ones_head", P), ("rot", P), ("cos", T), ("sin", T), ("strict", P), ("incl", P),
          ("causal_neg", P), ("decay_neg", P), ("levels", N_LEVELS * P), ("sel_pair", 2 * P), ("sel_head", 4 * P), ("eps", 4)]
CONSTS_2 = [("rot2", P), ("cos2", T), ("sin2", T)]
CONST_AT = {}
N_CONSTS = 0
for _name, _n in CONSTS:
    CONST_AT[_name] = N_CONSTS
    N_CONSTS += _n
CONST2_AT = {}
N_CONSTS_2 = 0
for _name, _n in CONSTS_2:
    CONST2_AT[_name] = N_CONSTS_2
    N_CONSTS_2 += _n
EPS_NORM, EPS_L2, EPS_GN, EPS_ONE = range(4)
GN_EPS = 64e-5
L2_EPS = 1e-12

NEG = -1e30
TAKEN = -3e38
TOPK = 128
ROW_WI, ROW_B, ROW_A = 0, 32, 64
DECAY = float(np.exp(-0.5))


def build_program(nc, io, out):
    run = [n for n, _ in PHASES]
    last_tile = max(BASE[n] + dict(PHASES)[n] for n in run)
    stream_tiles = -(-last_tile // RING) * RING
    with ExitStack() as ctx:
        def sb(name, shape, dt=F32):
            return ctx.enter_context(nc.sbuf_tensor(name, shape, dt))

        S = {}

        def sem(*names):
            for name in names:
                S[name] = ctx.enter_context(nc.semaphore(name))

        x = sb("x", [P, KD, T])
        consts = sb("consts", [P, N_CONSTS])
        params = sb("params", [P, N_PARAMS])
        w_hi = sb("w_hi", [P, RING, TILE], F32R)
        sil = sb("sil", [P, 2, T])
        sq = sb("sq", [P, 2, T])
        squares = (sq[:, 0, :], sq[:, 1, :], sil[:, 0, :], sil[:, 1, :])
        rtok = sb("rtok", [P, TB])
        head_tok = sb("head_tok", [P, 96])
        ada = sb("ada", [P, 2, ADA_TILES])
        gmod = sb("gmod", [P, 2, KD])
        stat = sb("stat", [P, 200])
        lora = sb("lora", [P, DEPTH, 2 * P])
        v_down = sb("v_down", [P, 2, 32])
        v_up = sb("v_up", [32, 2 * P])
        state = sb("state", [P, 4, HD])
        v_first = nc.dram_tensor("v_first", (2, P, T), F32, kind="Internal").ap()
        with nc.sbuf_tensor("w_raw", [P, RING, TILE], F32) as w_raw:
            pass
        w_lo = sb("w_lo", [P, RING, TILE], F32R)
        with nc.sbuf_tensor("core_mem", [P, 16, T], F32) as core_mem:
            pass
        h_hi = sb("h_hi", [P, KD, T], F32R)
        h_lo = sb("h_lo", [P, KD, T], F32R)
        with ExitStack() as ffn_scope:
            a_hi = ffn_scope.enter_context(nc.sbuf_tensor("a_hi", [P, NF, T], F32R))
            a_lo = ffn_scope.enter_context(nc.sbuf_tensor("a_lo", [P, NF, T], F32R))
            ada_raw = ffn_scope.enter_context(nc.sbuf_tensor("ada_raw", [P, 2, TILE], F32))
        with ExitStack() as mla_scope:
            def rounded(name, shape):
                return mla_scope.enter_context(nc.sbuf_tensor(name, shape, F32R))

            hc_hi, hc_lo = rounded("hc_hi", [P, KD, CTX]), rounded("hc_lo", [P, KD, CTX])
            cq_hi, cq_lo = rounded("cq_hi", [P, 3, T]), rounded("cq_lo", [P, 3, T])
            ckv_hi, ckv_lo = rounded("ckv_hi", [P, 2, TK]), rounded("ckv_lo", [P, 2, TK])
            mem2 = mla_scope.enter_context(nc.sbuf_tensor("mem2", [P, 28, T], F32))
        with ExitStack() as fourier_scope:
            g_hi = fourier_scope.enter_context(nc.sbuf_tensor("g_hi", [P, 16, T], F32R))
            g_lo = fourier_scope.enter_context(nc.sbuf_tensor("g_lo", [P, 16, T], F32R))
        mem = sb("mem", [P, 48, T])
        ps = ctx.enter_context(nc.psum_tensor("ps", [P, 8, T], F32))

        def const(name, lo=0, n=P):
            return consts[:, CONST_AT[name] + lo:CONST_AT[name] + lo + n]

        def param(name, c=0, n=1):
            return params[:, PARAM_AT[name] + c:PARAM_AT[name] + c + n]

        def cond_rows(n):
            rows = [sq[:, :, :].rearrange("p s t -> p (s t)")]
            if n == 0:
                rows.append(mem[:, 2 * NF - 2:2 * NF, :].rearrange("p s t -> p (s t)"))
            return rows

        def eps(which):
            return const("eps", which, 1)

        flat = mem[:, :, :].rearrange("p u t -> p (u t)")
        RW_AT, CONV_AT = 12 * T, 20 * T
        rw = flat[:, RW_AT:RW_AT + 7 * (T + 1)].rearrange("p (c t) -> p c t", t=T + 1)
        cv = flat[:, CONV_AT:CONV_AT + 6 * (T + 3)].rearrange("p (c t) -> p c t", t=T + 3)
        U_KI, U_QI, U_K, U_Q, U_V, U_MISC = 0, 2, 6, 7, 1, 11
        U_Z, U_Y = 27, 29


        def att_unit(m):
            return {1: U_MISC, 11: U_V}.get(m, m)


        def rec_out(m):
            if m < 7:
                return rw[:, m, 1:T + 1]
            if m < 13:
                return cv[:, m - 7, 3:T + 3]
            return mem[:, U_Z + m - 13, :]


        soft = mem[ROW_A:ROW_A + 4, 19, :]


        def blk(n):
            return slice(n * P, (n + 1) * P)


        def by_block(ap):
            return ap.rearrange("p c (n t) -> p c n t", t=P)


        def over_heads(mask):
            return mask.unsqueeze(1).to_broadcast([P, 4, P])


        def heads(ap):
            return ap.rearrange("p (h t) -> p h t", h=4)


        def evens(ap, level):
            return ap.rearrange("p (q two s) -> p q two s", two=2, s=1 << level)[:, :, 0, :]


        def odds(ap, level):
            return ap.rearrange("p (q two s) -> p q two s", two=2, s=1 << level)[:, :, 1, :]


        def compact(ap, level):
            return ap.rearrange("p (q s) -> p q s", s=1 << level)


        C_L, C_INV, C_INV_T, C_N, C_T1, C_A = 0, 2, 4, 8, 10, 12
        C_R, C_U = sil[:, 0, :], sil[:, 1, :]
        HALF = T // 2


        def inv_t_unit(n, g):
            return C_INV_T + 2 * (n % 2) + g


        S_PT, S_OUT, S_P, R_KK, R_SQ, G_CONV = 0, 2, 3, 5, 7, 9
        INDEX_ITEMS = [(n, h) for n in (3, 2, 1) for h in range(8)]
        INDEX_PER_TILE = 4
        FROM_LAST = (KD - 1, *range(KD - 1))
        ATT_ORDER = (0, 3, 2, 1)
        ITEMS = [(n, c, hh) for n in ATT_ORDER for c in range(4) for hh in range(2)]
        ST_WI, ST_TOP, ST_MAX, ST_SUM, ST_INV = 0, 32, 40, 72, 104
        ST_CM, ST_CE, ST_GAMMA, ST_OMKA, ST_GNEG, ST_GLAST, ST_EGL, ST_EA = 112, 120, 128, 136, 138, 154, 162, 170

        flat2 = mem2[:, :, :].rearrange("p u t -> p (u t)")
        ctx_x = flat2[:, 0:KD * CTX].rearrange("p (k t) -> p k t", k=KD)
        cq = mem2[:, 4:7, :]
        ckv = flat2[:, 7 * T:7 * T + 2 * TK].rearrange("p (c t) -> p c t", c=2)
        kpe = flat2[:, 10 * T:10 * T + TK]
        vtok = mem2[:, 4:10, :]
        CQ_STD, CKV_STD, CTX_STD = 20, 23, 26
        ctx_sq = flat2[:, 12 * T:12 * T + KD * CTX].rearrange("p (k t) -> p k t", k=KD)
        ckv_sq = flat2[:, CKV_STD * T:CKV_STD * T + 2 * TK].rearrange("p (c t) -> p c t", c=2)
        z_conv = flat2[:, 2 * T:2 * T + T + 2]
        Y_CONV, Y_MLA, Q_MLA, O_MLA = 12, 16, 20, 3
        kmla = core_mem[:, 0:12, :].rearrange("p u t -> p (u t)").rearrange("p (h t) -> p h t", h=8)
        consts2 = core_mem[:, 12:15, :].rearrange("p u t -> p (u t)")[:, 0:N_CONSTS_2]
        probs = [flat2[:, s * TK:(s + 1) * TK] for s in range(2)]
        wide = [sil[:, :, :].rearrange("p s t -> p (s t)")[:, 0:TK], sq[:, :, :].rearrange("p s t -> p (s t)")[:, 0:TK]]
        psf = ps[:, :, :].rearrange("p b t -> p (b t)")
        PE_ROWS = slice(HD, QKD)
        KB = TK // P


        def qk_width(i):
            return T if i < 8 else TK


        def qk_tok(i):
            return head_tok[:, KB * (i % 2):KB * (i % 2) + qk_width(i) // P]




        def const2(name, n):
            return consts2[:, CONST2_AT[name]:CONST2_AT[name] + n]


        def ada_col(layer, part, k, which=0):
            q = (6 * layer + part) * KD + k
            return ada[:, which, q:q + 1]


        def ada_cols(layer, part, which=0):
            q = (6 * layer + part) * KD
            return ada[:, which, q:q + KD]

        x_loaded = [ctx.enter_context(nc.semaphore(f"x_loaded{s}")) for s in range(2)]
        w_loaded = [ctx.enter_context(nc.semaphore(f"w_loaded{s}")) for s in range(RING)]
        ada_loaded = [ctx.enter_context(nc.semaphore(f"ada_loaded{s}")) for s in range(2)]
        sem("basics_loaded", "consts_loaded", "w_hi_ready", "w_lo_ready", "w_used", "out_stored")
        sem("sq_ready", "ss_ready", "std_ready", "rtok_ready", "rstd_ready", "hf_ready", "h_hi_ready", "h_ready", "x_ready")
        sem("silu_ready", "af_ready", "a_hi_ready", "a_ready", "down_added")
        sem("cond_loaded", "cond_ready", "ada_used")
        sem("dve_order", "act_order")
        sem("proj_out", "rot_ready", "roped", "head_sq", "head_sum", "head_std", "head_inv", "head_spread", "head_done")
        sem("wi_ready", "v_ready", "v_out", "index_ready", "relu_ready", "score_added", "bonus_taken")
        sem("s_ready", "score_taken", "max_ready", "p_ready", "p_turned", "pt_out", "pv_done", "o_taken", "ot_ready", "y_att_out")
        sem("shifted", "lora_in", "lora_ready", "gates_ready", "decay_in", "decay_ready", "kk_in", "vf_moved", "vd_ready", "vd_out",
            "vu_ready", "v_gate", "bonus_in", "bonus_sum", "rwkv_ready", "turned", "turned_out")
        sem("conv_ready", "conv_act", "sp_in", "sp_exp", "sp_ln", "g_ready", "beta_ready", "g_turned", "g_taken", "spread_ready", "spread_taken", "eg_ready", "dt_ready",
            "kd_ready", "gdn_ready")
        sem("gram_ready", "gram_taken", "n_ready", "t1_ready", "t1_out", "dx_ready", "inv_ready", "a_gram_ready", "a_gram_out",
            "r_ready", "r_out", "u_ready", "u_out", "y_ready", "y_out", "s_next", "s_out")
        sem("mean_ready", "centred")
        sem("ctx_loaded", "consts2_loaded", "ctx_sq", "ctx_sum", "ctx_std", "ctx_f", "ctx_hi", "ctx_ready", "ctx_out",
            "lat_sq", "lat_sum", "lat_std", "lat_f", "lat_hi", "lat_ready", "c_out", "u_taken", "conv_taken",
            "qk_ready", "qk_out", "qk_sq", "qk_sum", "qk_std", "qk_inv", "qk_spread", "qk_done", "lat_inv", "lat_spread", "kpe_ready", "rot2_ready", "rot2_done", "vtok_ready", "vtok_out",
            "g_done", "g_hi_ready", "g_split")

        block = ctx.enter_context(nc.Block())

        @block.sync
        def _(sp):
            first, last = 2 * P, CONST_AT["eps"]
            half = KD // 2
            x_t = io["x_t"].rearrange("(k p) t -> p k t", p=P)
            sp.dma_start(x[:, 0:half, :], x_t[:, 0:half, :]).then_inc(x_loaded[0], 16)
            sp.dma_start(consts[:, 0:first], io["consts"][:, 0:first]).then_inc(S["basics_loaded"], 16)
            sp.dma_start(consts[:, last:], io["consts"][:, last:]).then_inc(S["basics_loaded"], 16)
            sp.dma_start(params[:, :], io["params"]).then_inc(S["basics_loaded"], 16)
            sp.dma_start(x[:, half:, :], x_t[:, half:, :]).then_inc(x_loaded[1], 16)
            for s in range(RING):
                sp.dma_start(w_raw[:, s, :], io["tiles"][s]).then_inc(w_loaded[s], 16)
            sp.dma_start(consts[:, first:last], io["consts"][:, first:last]).then_inc(S["consts_loaded"], 16)
            sp.dma_start(lora[:, :, :], io["lora"].rearrange("l p n -> p l n")).then_inc(S["consts_loaded"], 16)
            sp.dma_start(v_down[:, :, :], io["v_down"].rearrange("(c p) n -> p c n", p=P)).then_inc(S["consts_loaded"], 16)
            sp.dma_start(v_up[:, :], io["v_up"]).then_inc(S["consts_loaded"], 16)
            with sp.Fori(1, stream_tiles // RING) as i:
                for s in range(RING):
                    sp.wait_ge(S["w_used"], RING * i + (s + 1 - RING))
                    sp.dma_start(w_raw[:, s, :], io["tiles"][RING * i + s]).then_inc(w_loaded[s], 16)
            sp.wait_ge(S["x_ready"], KD * sum(n.startswith("ffn") or n.endswith("_out") or "mix_out" in n for n in run))
            sp.dma_start(out.rearrange("(k p) t -> p k t", p=P), x[:, :, :]).then_inc(S["out_stored"], 16)
            sp.wait_ge(S["vf_moved"], 16)
            sp.wait_ge(S["out_stored"], 16)

        @block.gpsimd
        def _(pool):
            with pool.Fori(0, stream_tiles // RING) as i:
                for s in range(RING):
                    pool.wait_ge(S["w_hi_ready"], RING * i + (s + 1))
                    nc.gpsimd.tensor_tensor(w_lo[:, s, :], w_raw[:, s, :], w_hi[:, s, :].bitcast(F32),
                                            ALU.subtract).then_inc(S["w_lo_ready"], 1)

        @block.scalar
        def _(act):
            seen = {}

            def due(name, n=1):
                seen[name] = seen.get(name, 0) + n
                return seen[name]

            def link(ins):
                ins.then_inc(S["act_order"], 1)
                act.wait_ge(S["act_order"], due("act_order"))

            def round_tile(t, i=None, step=RING):
                if i is None and t >= stream_tiles:
                    return
                turn = t // RING + 1
                act.wait_ge(w_loaded[t % RING], 16 * turn if i is None else 16 * i + 16 * turn)
                nc.scalar.activation(w_hi[:, t % RING, :], w_raw[:, t % RING, :], ACT.Copy).then_inc(S["w_hi_ready"], 1)

            def square_x(n, k, updates):
                if updates:
                    act.wait_ge(S["x_ready"], KD * (updates - 1) + n + 1)
                else:
                    act.wait_ge(x_loaded[k // (KD // 2)], 16)
                if due("sq_slot") > len(squares):
                    act.wait_ge(S["ss_ready"], seen["sq_slot"] - len(squares))
                nc.scalar.activation(squares[n % len(squares)], x[:, k, :], ACT.Square).then_inc(S["sq_ready"], 1)

            def norm_x(order, updates, between=None, shift=None):
                for n in range(seen.pop("early", 0), KD):
                    square_x(n, order[n], updates)
                    if not updates and 3 <= n < 5:
                        round_tile(n - 3)
                if between:
                    between()
                act.wait_ge(S["ss_ready"], seen["sq_slot"])
                nc.scalar.activation(rtok[:, :], ps[:, 7, 0:TB], ACT.Sqrt, scale=1.0 / D, bias=eps(EPS_NORM)).then_inc(S["std_ready"], 1)
                for t in seen.pop("late_tiles"):
                    round_tile(t)
                round_h(range(KD), shift)

            def round_out(base, updates):
                for k in range(KD - 1):
                    round_tile(base + k + 4)
                    if k:
                        square_x(k - 1, k - 1, updates + 1)
                seen["early"] = KD - 2
                seen["late_tiles"] = [base + KD - 1 + 4]

            def round_h(chunks, shift=None):
                for k in chunks:
                    act.wait_ge(S["hf_ready"], due("hf_ready"))
                    if shift is None:
                        ins = nc.scalar.activation(h_hi[:, k, :], sil[:, k % 2, :], ACT.Copy)
                    else:
                        ins = nc.scalar.activation(h_hi[:, k, :], sil[:, k % 2, :], ACT.Identity, bias=shift(k))
                    ins.then_inc(S["h_hi_ready"], 1)

            def load_ada(q):
                act.dma_start(ada_raw[:, q % 2, :], io["ada_tiles"][q]).then_inc(ada_loaded[q % 2], 16)

            def ffn(n, order, updates, shift=None):
                base = BASE[f"ffn{n}"]
                norm_x(order, updates, shift=shift)
                if n < 4:
                    for c, row in enumerate(cond_rows(n)):
                        act.dma_start(row, io["cond"][c].partition_broadcast(P)).then_inc(S["cond_loaded"], 16)
                        loaded = due("cond_loaded", 16)
                    load_ada(ADA_PER_FFN * n)
                    act.wait_ge(S["cond_loaded"], loaded)
                    for row in cond_rows(n):
                        nc.scalar.activation(row, row, ACT.Silu).then_inc(S["cond_ready"], 1)
                with act.Fori(0, NF // 2) as i:
                    for j in range(2):
                        act.wait_ge(S["w_used"], base + 4 * i + (2 * j + 2))
                        act.wait_ge(S["a_ready"], NF * n + 2 * i + (j + 1))
                        nc.scalar.activation(sil[:, j, :], ps[:, 2 * j, :], ACT.Silu).then_inc(S["silu_ready"], 1)
                        round_tile(base + 4 + 2 * j, i)
                        round_tile(base + 5 + 2 * j, i)
                        if n < 4:
                            act.wait_ge(S["ada_used"], ADA_PER_FFN * n + 2 * i + (j + 1))
                            act.dma_start(ada_raw[:, 1 - j, :], io["ada_tiles"][2 * i + (ADA_PER_FFN * n + j + 1)]).then_inc(ada_loaded[1 - j], 16)
                        act.wait_ge(S["af_ready"], NF * n + 2 * i + (j + 3))
                        nc.scalar.activation(a_hi[:, 2 * i + j, :], sil[:, j, :], ACT.Copy).then_inc(S["a_hi_ready"], 1)
                if n < 4:
                    act.wait_ge(S["ada_used"], ADA_PER_FFN * n + NF + 1)
                    load_ada(ADA_PER_FFN * n + NF + 1)
                down = base + 2 * NF
                for t in range(down, down + 2):
                    round_tile(t + 4)
                with act.Fori(0, 2) as i:
                    for r in range(RING):
                        round_tile(down + 6 + r, i)
                for t in range(down + 10, down + 13):
                    round_tile(t + 4)
                if n < 2 * DEPTH + 1:
                    if n < 4:
                        act.wait_ge(S["ada_used"], ADA_PER_FFN * (n + 1) + 1)
                    for c in range(KD // 2):
                        square_x(c, FFN_ORDER[c], updates + 1)
                    seen["early"] = KD // 2
                for t in range(down + 13, down + NF - 1):
                    round_tile(t + 4)
                seen["late_tiles"] = [down + NF - 1 + 4]

            act.wait_ge(S["basics_loaded"], 48)
            seen["late_tiles"] = range(2, RING)
            def head_roots(bank, chunks, scale, which_eps):
                act.wait_ge(S["head_sum"], due("head_sum"))
                n = 2 * TB * chunks
                nc.scalar.activation(head_tok[:, 0:n], ps[:, bank, 0:n], ACT.Sqrt, scale=scale, bias=eps(which_eps)).then_inc(S["head_std"], 1)


            def attention(l, order, updates):
                base = BASE[f"att_in{l}"]
                norm_x(order, updates)
                for m in range(ATT_TILES):
                    act.wait_ge(S["w_used"], base + m + 1)
                    nc.scalar.activation(mem[:, att_unit(m), :], ps[:, m % 2, :], ACT.Copy).then_inc(S["proj_out"], 1)
                    round_tile(base + m + 4)
                    done = due("proj_out")
                    if U_K <= m < U_K + 5:
                        act.wait_ge(S["proj_out"], done)
                        nc.scalar.activation(mem[:, 33 + m - U_K, :], mem[:, m, :], ACT.Square).then_inc(S["head_sq"], 1)
                base = BASE[f"rec_in{l}"]
                for m in range(REC_TILES):
                    if m == REC_TILES - 2:
                        lg = rw[:, 6, 1:T + 1]
                        act.wait_ge(S["shifted"], l + 1)
                        nc.scalar.activation(lg[0:32, :], lg[0:32, :], ACT.Tanh)
                        nc.scalar.activation(lg[64:128, :], lg[64:128, :], ACT.Sigmoid).then_inc(S["lora_in"], 1)
                    act.wait_ge(S["w_used"], base + m + 1)
                    nc.scalar.activation(rec_out(m), ps[:, m % 2, :], ACT.Copy).then_inc(S["proj_out"], 1)
                    if m == 0:
                        act.wait_ge(S["v_ready"], l + 1)
                        nc.scalar.activation(mem[:, 45, :], ps[:, 7, :], ACT.Copy).then_inc(S["v_out"], 1)
                    for n, h in INDEX_ITEMS[INDEX_PER_TILE * m:INDEX_PER_TILE * (m + 1)]:
                        i = due("relu") - 1
                        w = (n + 1) * P
                        act.wait_ge(S["index_ready"], i + 1)
                        if i >= 2:
                            act.wait_ge(S["score_added"], i - 1)
                        nc.scalar.activation(mem[:, 43 + i % 2, 0:w], ps[:, 2 + i % 2, 0:w], ACT.Relu).then_inc(S["relu_ready"], 1)
                    if m == 1:
                        head_roots(4, 5, 1.0 / HD, EPS_NORM)
                    round_tile(base + m + 4)
                if l == 0:
                    act.dma_start(v_first.rearrange("c p t -> p c t"), rw[:, 4:6, 1:T + 1]).then_inc(S["vf_moved"], 16)
                act.wait_ge(S["lora_ready"], l + 1)
                for c in range(2):
                    nc.scalar.activation(mem[:, c, :], ps[:, 2 + c, :], ACT.Sigmoid, bias=param(f"w0{l}", c))
                    nc.scalar.activation(mem[:, 2 + c, :], ps[:, 4 + c, :], ACT.Sigmoid, bias=param(f"a0{l}", c))
                    ins = nc.scalar.activation(mem[:, 43 + c, :], ps[:, 6 + c, :], ACT.Copy)
                ins.then_inc(S["gates_ready"], 1)
                beta = mem[ROW_B:ROW_B + 4, U_MISC, :]
                nc.scalar.activation(beta, beta, ACT.Sigmoid).then_inc(S["beta_ready"], 1)

                def meanwhile(i):
                    if i == 1:
                        act.wait_ge(S["kk_in"], l + 1)
                        nc.scalar.activation(core_mem[:, R_SQ:R_SQ + 2, :], core_mem[:, R_KK:R_KK + 2, :], ACT.Square).then_inc(S["head_sq"], 1)
                    if i == 3:
                        act.wait_ge(S["decay_in"], l + 1)
                        nc.scalar.activation(mem[:, 33:35, :], mem[:, 4:6, :], ACT.Exp, scale=-DECAY)
                        nc.scalar.activation(mem[:, 35:37, :], mem[:, 0:2, :], ACT.Exp, scale=-DECAY)
                        nc.scalar.activation(mem[:, 37:39, :], mem[:, 4:6, :], ACT.Exp, scale=DECAY)
                        nc.scalar.activation(stat[:, ST_GAMMA:ST_GAMMA + 8], stat[:, ST_GAMMA:ST_GAMMA + 8], ACT.Exp, scale=-DECAY)
                        nc.scalar.activation(stat[ROW_A:ROW_A + 4, ST_EA:ST_EA + 1], param(f"a_log{l}")[ROW_A:ROW_A + 4, :], ACT.Exp).then_inc(S["decay_ready"], 1)
                    if i == 4:
                        head_roots(0, 2, 1.0, EPS_L2)
                    if i == 31:
                        act.wait_ge(S["sp_in"], l + 1)
                        nc.scalar.activation(soft, soft, ACT.Exp).then_inc(S["sp_exp"], 1)

                due("proj_out", REC_TILES)
                i0 = seen.get("items", 0)
                for i in range(len(ITEMS) + 1):
                    meanwhile(i)
                    if i < len(ITEMS):
                        w = (ITEMS[i][0] + 1) * P
                        p = core_mem[:, S_P + i % 2, 0:w]
                        act.wait_ge(S["max_ready"], i0 + i + 1)
                        nc.scalar.activation(p, p, ACT.Exp, bias=stat[:, ST_MAX + i:ST_MAX + i + 1], accum_out=stat[:, ST_SUM + i:ST_SUM + i + 1]).then_inc(S["p_ready"], 1)
                    if i >= 1:
                        w = (ITEMS[i - 1][0] + 1) * P
                        act.wait_ge(S["p_turned"], i0 + i)
                        if i >= 3:
                            act.wait_ge(S["pv_done"], i0 + i - 2)
                        nc.scalar.activation(core_mem[:, S_PT + (i - 1) % 2, 0:w], ps[:, 4 + (i - 1) % 2, 0:w], ACT.Copy).then_inc(S["pt_out"], 1)
                    if i % 8 == 2 and i > 2:
                        outputs_out()
                outputs_out()
                due("items", len(ITEMS))


            def outputs_out():
                t = due("ot") - 1
                n = ATT_ORDER[t % TB]
                act.wait_ge(S["ot_ready"], t + 1)
                nc.scalar.activation(mem[:, U_Y:U_Y + 4, blk(n)], heads(ps[:, 7, :]), ACT.Copy).then_inc(S["y_att_out"], 1)


            def turn_out(dest):
                n = due("turned")
                act.wait_ge(S["turned"], n)
                nc.scalar.activation(dest, ps[:, n % 2, :], ACT.Copy).then_inc(S["turned_out"], 1)


            def recurrences(l, updates):
                act.wait_ge(S["sp_exp"], l + 1)
                nc.scalar.activation(soft, soft, ACT.Ln, bias=eps(EPS_ONE)[ROW_A:ROW_A + 4, :]).then_inc(S["sp_ln"], 1)
                if l > 0:
                    act.wait_ge(S["vf_moved"], 16)
                    act.wait_ge(S["y_att_out"], TB * (l + 1))
                    act.dma_start(mem[:, 9:11, :], v_first.rearrange("c p t -> p c t")).then_inc(S["vf_moved"], 16)
                    act.wait_ge(S["vd_ready"], 1)
                    nc.scalar.activation(mem[0:32, 45, :], ps[0:32, 6, :], ACT.Copy).then_inc(S["vd_out"], 1)
                    act.wait_ge(S["vu_ready"], 1)
                    for c in range(2):
                        ins = nc.scalar.activation(core_mem[:, R_SQ + c, :], ps[:, 7 - c, :], ACT.Sigmoid, bias=param("v0", c))
                    ins.then_inc(S["v_gate"], 1)
                act.wait_ge(S["conv_ready"], l + 1)
                act.wait_ge(S["rwkv_ready"], l + 1)
                nc.scalar.activation(mem[:, 33:37, :], core_mem[:, G_CONV:G_CONV + 4, :], ACT.Silu).then_inc(S["conv_act"], 1)
                act.wait_ge(S["conv_act"], l + 1)
                for pair in range(2):
                    nc.scalar.activation(mem[:, 39 + 2 * pair:41 + 2 * pair, :], mem[:, 33 + 2 * pair:35 + 2 * pair, :], ACT.Square).then_inc(S["head_sq"], 1)
                nc.scalar.activation(mem[:, 37:39, :], core_mem[:, G_CONV + 4:G_CONV + 6, :], ACT.Silu)
                nc.scalar.activation(mem[:, U_Z:U_Z + 2, :], mem[:, U_Z:U_Z + 2, :], ACT.Silu)
                head_roots(2, 4, 1.0, EPS_NORM)
                if l == 0:
                    due("turned", 6)
                else:
                    for u in (0, 1, 4, 5, 2, 3):
                        turn_out(mem[:, u, :])
                act.wait_ge(S["spread_taken"], 3 * l + 1)
                nc.scalar.activation(mem[:, 41:43, :], ps[:, 2:4, :], ACT.Exp).then_inc(S["eg_ready"], 1)
                for c in range(2):
                    for n in range(TB):
                        at = ST_GLAST + TB * c + n
                        ins = nc.scalar.activation(mem[:, 24 + c, blk(n)], ps[:, 2 + c, blk(n)], ACT.Exp, scale=-1.0, bias=stat[:, at:at + 1])
                ins.then_inc(S["eg_ready"], 1)
                for u in (26, 19):
                    turn_out(mem[:, u, :])
                act.wait_ge(S["spread_taken"], 3 * l + 3)
                nc.scalar.activation(mem[:, 20:24, :], mem[:, 20:24, :], ACT.Exp).then_inc(S["dt_ready"], 1)
                for u in (45, 6):
                    turn_out(mem[:, u, :])
                for n in range(TB + 1):
                    core_step(l, n)
                post(l, updates)


            def core_step(l, n):
                b = TB * l + n
                for lev in range(1, N_LEVELS):
                    if n < TB:
                        for g in range(2):
                            act.wait_ge(S["t1_ready"], 2 * (N_LEVELS * b + lev) + g + 1)
                            nc.scalar.activation(core_mem[:, C_T1 + g, :], ps[:, 2 + g, :], ACT.Copy).then_inc(S["t1_out"], 1)
                    if n == 0:
                        continue
                    if lev == 2:
                        act.wait_ge(S["r_ready"], b)
                        nc.scalar.activation(C_R.rearrange("p (g t) -> p g t", g=2), ps[:, 6:8, 0:HALF], ACT.Copy).then_inc(S["r_out"], 1)
                    if lev == 3:
                        act.wait_ge(S["u_ready"], b)
                        nc.scalar.activation(C_U, ps[:, 0, :], ACT.Copy).then_inc(S["u_out"], 1)
                    if lev == 5:
                        act.wait_ge(S["y_ready"], b)
                        at = (n - 1) * P
                        nc.scalar.activation(rw[:, 0:2, 1 + at:1 + at + P], heads(ps[:, 6, :])[:, 0:2, :], ACT.Copy)
                        nc.scalar.activation(mem[:, 37:39, blk(n - 1)], heads(ps[:, 6, :])[:, 2:4, :], ACT.Copy).then_inc(S["y_out"], 1)


            def post(l, updates):
                act.wait_ge(S["y_out"], TB * (l + 1))
                nc.scalar.activation(mem[:, 35:37, :], mem[:, 37:39, :], ACT.Square).then_inc(S["head_sq"], 1)
                act.wait_ge(S["centred"], l + 1)
                nc.scalar.activation(mem[:, 33:35, :], rw[:, 0:2, 1:T + 1], ACT.Square).then_inc(S["head_sq"], 1)
                round_h((0, 1))
                head_roots(4, 2, 1.0 / HD, EPS_NORM)
                round_h((2, 3))
                act.wait_ge(S["head_spread"], due("head_spread"))
                head_roots(2, 2, 1.0 / HD, EPS_GN)
                round_h(range(4, KD))
                round_out(BASE[f"mix_out{l}"], updates)


            def mla(order, updates):
                base = BASE["mla_in"]

                def load_ctx():
                    act.wait_ge(S["x_ready"], KD * updates)
                    act.dma_start(ctx_x, io["ctx_t"].rearrange("(k p) t -> p k t", p=P)).then_inc(S["ctx_loaded"], 16)

                norm_x(order, updates, load_ctx, lambda k: ada_col(0, 0, k))
                act.wait_ge(S["ctx_loaded"], 16)
                nc.scalar.activation(ctx_sq, ctx_x, ACT.Square).then_inc(S["ctx_sq"], 1)
                for m in range(6):
                    if m == 2:
                        act.wait_ge(S["ctx_sum"], 1)
                        nc.scalar.activation(mem2[:, CTX_STD, 0:CTX], ps[:, 6, 0:CTX], ACT.Sqrt, scale=1.0 / D, bias=eps(EPS_NORM)).then_inc(S["ctx_std"], 1)
                        act.wait_ge(S["ctx_f"], 1)
                        nc.scalar.activation(hc_hi[:, :, :], ctx_x, ACT.Copy).then_inc(S["ctx_hi"], 1)
                    act.wait_ge(S["w_used"], base + m + 1)
                    bank = ps[:, m % 2, :]
                    out = cq[:, m, :] if m < 3 else ckv[:, m - 3, 0:T] if m < 5 else kpe[:, 0:T]
                    nc.scalar.activation(out, bank, ACT.Copy).then_inc(S["proj_out"], 1)
                    if m >= 3:
                        out = ckv[:, m - 3, T:TK] if m < 5 else kpe[:, T:TK]
                        nc.scalar.activation(out, ps[:, 2 + m % 2, 0:CTX], ACT.Copy).then_inc(S["ctx_out"], 1)
                    round_tile(base + m + 4)
                act.wait_ge(S["proj_out"], due("proj_out", 6))
                act.wait_ge(S["ctx_out"], 3)
                nc.scalar.activation(mem2[:, CQ_STD:CQ_STD + 3, :], cq, ACT.Square).then_inc(S["lat_sq"], 1)
                nc.scalar.activation(ckv_sq, ckv, ACT.Square).then_inc(S["lat_sq"], 1)

                def conv_tile(m):
                    act.wait_ge(S["w_used"], base + m + 1)
                    j, part = (m - 6) // 3, (m - 6) % 3
                    if part == 0:
                        if j >= 2:
                            act.wait_ge(S["u_taken"], j - 1)
                        nc.scalar.activation(mem2[:, j % 2, :], ps[:, 0, :], ACT.Copy).then_inc(S["c_out"], 1)
                    round_tile(base + m + 4)

                conv_tile(6)
                act.wait_ge(S["lat_sum"], 1)
                nc.scalar.activation(head_tok[:, 0:TB], ps[:, 4, 0:TB], ACT.Sqrt, scale=1.0 / 384, bias=eps(EPS_NORM))
                nc.scalar.activation(head_tok[:, TB:TB + KB], ps[:, 4, TB:TB + KB], ACT.Sqrt, scale=1.0 / 256, bias=eps(EPS_NORM)).then_inc(S["lat_std"], 1)
                conv_tile(7)
                conv_tile(8)
                act.wait_ge(S["lat_f"], 1)
                nc.scalar.activation(cq_hi[:, :, :], cq, ACT.Copy).then_inc(S["lat_hi"], 1)
                act.wait_ge(S["lat_f"], 2)
                nc.scalar.activation(ckv_hi[:, :, :], ckv, ACT.Copy).then_inc(S["lat_hi"], 1)
                for m in range(9, 18):
                    conv_tile(m)
                act.dma_start(consts2, io["consts_2"]).then_inc(S["consts2_loaded"], 16)

                def qk(i):
                    last_of_tile = i % 2 if i < 8 else i % 4 == 3
                    if last_of_tile:
                        t = BASE["mla_q"] + i // 2 if i < 8 else BASE["mla_kv"] + (i - 8) // 4
                        act.wait_ge(S["w_used"], t + 1)
                    else:
                        act.wait_ge(S["qk_ready"], due("qk_ready"))
                    b = 2 * (i % 2)
                    if i < 8:
                        head, width = mem2[0:QKD, Q_MLA + i, :], T
                        nc.scalar.activation(head, ps[0:QKD, b, :], ACT.Copy).then_inc(S["qk_out"], 1)
                    else:
                        head, width = kmla[0:QKD, i - 8, :], TK
                        nc.scalar.activation(head[0:HD, :], psf[0:HD, b * T:b * T + TK], ACT.Copy).then_inc(S["qk_out"], 1)
                        act.wait_ge(S["kpe_ready"], 1)
                    if last_of_tile:
                        round_tile(t + 4)
                    if i >= 2:
                        act.wait_ge(S["qk_sum"], i - 1)
                    act.wait_ge(S["qk_out"], i + 1)
                    nc.scalar.activation(wide[i % 2][0:QKD, 0:width], head, ACT.Square).then_inc(S["qk_sq"], 1)

                def qk_std(i):
                    act.wait_ge(S["qk_sum"], i + 1)
                    if i >= 2:
                        act.wait_ge(S["qk_spread"], i - 1)
                    nc.scalar.activation(qk_tok(i), ps[:, 6, 0:qk_width(i) // P], ACT.Sqrt, scale=1.0 / QKD, bias=eps(EPS_NORM)).then_inc(S["qk_std"], 1)

                for i in range(16):
                    qk(i)
                    if i:
                        qk_std(i - 1)
                qk_std(15)
                t = BASE["mla_kv"] + 2
                for n in range(6):
                    if n < 5:
                        act.wait_ge(S["vtok_ready"], n + 1)
                    else:
                        act.wait_ge(S["w_used"], t + 1)
                    nc.scalar.activation(vtok[:, n, :], ps[:, n % 4, :], ACT.Copy).then_inc(S["vtok_out"], 1)
                round_tile(t + 4)
                i0 = seen["items"]
                scale = float(QKD ** -0.5)
                for i in range(32):
                    act.wait_ge(S["max_ready"], i0 + i + 1)
                    if i >= 2:
                        act.wait_ge(S["p_turned"], i0 + i - 1)
                    at = 2 * (i % 2) * T
                    nc.scalar.activation(probs[i % 2], psf[:, at:at + TK], ACT.Exp, scale=scale, bias=stat[:, ST_MAX + i:ST_MAX + i + 1],
                                         accum_out=stat[:, ST_SUM + i:ST_SUM + i + 1]).then_inc(S["p_ready"], 1)
                    if i % 8 == 2 and i > 2:
                        mla_outputs_out()
                mla_outputs_out()
                due("items", 32)
                round_h(range(KD))
                round_out(BASE["mla_out"], updates)


            def mla_outputs_out():
                t = due("ot") - 1
                act.wait_ge(S["ot_ready"], t + 1)
                nc.scalar.activation(mem2[:, Y_MLA:Y_MLA + 4, blk(t % TB)], heads(ps[:, 7, :]), ACT.Copy).then_inc(S["y_att_out"], 1)


            def fourier(order, updates):
                norm_x(order, updates, shift=lambda k: ada_col(1, 0, k))
                t = BASE["dft_group"]
                for i in range(16):
                    if i < 15:
                        act.wait_ge(S["g_done"], i + 1)
                    else:
                        act.wait_ge(S["w_used"], t + 1)
                    nc.scalar.activation(g_hi[:, i, :], ps[:, i % 4, :], ACT.Copy).then_inc(S["g_hi_ready"], 1)
                round_tile(t + 4)
                for m in range(4):
                    round_tile(BASE["dft_time"] + m + 4)
                round_h(FROM_LAST)
                round_out(BASE["fourier_out"], updates)
            updates, order = 0, range(KD)
            for name in run:
                l = int(name[-1]) if name[-1].isdigit() else None
                if name.startswith("ffn"):
                    ffn(l, order, updates, (lambda k: ada_col(l - 4, 3, k)) if l >= 4 else None)
                    updates, order = updates + 1, FFN_ORDER
                if name == "ffn0":
                    act.wait_ge(S["consts_loaded"], 64)
                if name.startswith("rec_in"):
                    attention(l, order, updates)
                if name.startswith("mix_out"):
                    recurrences(l, updates)
                    updates, order = updates + 1, range(KD)
                if name == "mla_out":
                    mla(order, updates)
                    updates, order = updates + 1, range(KD)
                if name == "fourier_out":
                    fourier(order, updates)
                    updates, order = updates + 1, range(KD)

        @block.vector
        def _(dve):
            seen = {}

            def due(name, n=1):
                seen[name] = seen.get(name, 0) + n
                return seen[name]

            def link(ins):
                ins.then_inc(S["dve_order"], 1)
                dve.wait_ge(S["dve_order"], due("dve_order"))

            def split_h(chunks, make, shift=None):
                todo, before = None, seen.get("h_hi_ready", 0)
                for n, k in enumerate(list(chunks) + [None]):
                    if k is not None:
                        if n >= 2:
                            dve.wait_ge(S["h_ready"], before + n - 1)
                        make(k, sil[:, k % 2, :]).then_inc(S["hf_ready"], 1)
                    if todo is not None:
                        dve.wait_ge(S["h_hi_ready"], due("h_hi_ready"))
                        slot, hi = sil[:, todo % 2, :], h_hi[:, todo, :].bitcast(F32)
                        if shift is None:
                            ins = nc.vector.tensor_tensor(h_lo[:, todo, :], slot, hi, ALU.subtract)
                        else:
                            ins = nc.vector.scalar_tensor_tensor(h_lo[:, todo, :], slot, shift(todo), hi, ALU.add, ALU.subtract)
                        ins.then_inc(S["h_ready"], 1)
                    todo = k

            def norm_x(gain, shift=None):
                dve.wait_ge(S["std_ready"], due("std_ready"))
                nc.vector.reciprocal(rtok[:, :], rtok[:, :]).then_inc(S["rtok_ready"], 1)
                dve.wait_ge(S["rstd_ready"], due("rstd_ready"))

                def make(k, slot):
                    return nc.vector.scalar_tensor_tensor(slot, x[:, k, :], gain(k), ps[:, 7, :], ALU.mult, ALU.mult)

                split_h(range(KD), make, shift)

            def ada_tile(n, r, i, conditions):
                dve.wait_ge(S["cond_ready"], seen["cond_ready"])
                dve.wait_ge(ada_loaded[r], 16 * i + 16 * (ADA_PER_FFN // 2 * n + 1))
                raw = ada_raw[:, r, :]
                at = 2 * i + (ADA_PER_FFN * n + r)
                column = slice(at, at + 1) if isinstance(i, int) else bass.ds(at, 1)
                if conditions == 2:
                    spare = mem[:, 2 * NF - 4:2 * NF - 2, :].rearrange("p s t -> p (s t)")
                    nc.vector.scalar_tensor_tensor(spare, raw, 1.0, cond_rows(n)[1], ALU.mult, ALU.mult, accum_out=ada[:, 1, column])
                nc.vector.scalar_tensor_tensor(raw, raw, 1.0, cond_rows(n)[0], ALU.mult, ALU.mult, accum_out=ada[:, 0, column]).then_inc(S["ada_used"], 1)

            def ffn(n, gain, shift, gate):
                base = BASE[f"ffn{n}"]
                norm_x(gain, shift)
                both = ADA_CTX // 2 if n == 0 else 0
                if n < 4:
                    seen["cond_ready"] = seen.get("cond_ready", 0) + len(cond_rows(n))

                def activations(i, conditions):
                    for j in range(2):
                        dve.wait_ge(S["silu_ready"], NF * n + 2 * i + (j + 1))
                        nc.vector.tensor_tensor(sil[:, j, :], sil[:, j, :], ps[:, 2 * j + 1, :], ALU.mult).then_inc(S["af_ready"], 1)
                        dve.wait_ge(S["a_hi_ready"], NF * n + 2 * i + (j + 1))
                        nc.vector.tensor_tensor(a_lo[:, 2 * i + j, :], sil[:, j, :], a_hi[:, 2 * i + j, :].bitcast(F32),
                                                ALU.subtract).then_inc(S["a_ready"], 1)
                        if n < 4:
                            ada_tile(n, j, i, conditions)

                if both:
                    with dve.Fori(0, both) as i:
                        activations(i, 2)
                with dve.Fori(both, NF // 2) as i:
                    activations(i, 1)
                if n < 4:
                    for j in range(ADA_PER_FFN - NF):
                        ada_tile(n, j, NF // 2, 1)
                    lo = ADA_PER_FFN * n
                    dve.wait_ge(S["ada_used"], lo + ADA_PER_FFN + 1)
                    for c, tiles in ((0, ADA_PER_FFN), (1, 2 * both)):
                        if tiles:
                            ins = nc.vector.tensor_tensor(ada[:, c, lo:lo + tiles], ada[:, c, lo:lo + tiles], param("ada_b", lo, tiles), ALU.add)
                    link(ins)
                for half in (1, 0):
                    for d, k in enumerate(FFN_ORDER[4 - 4 * half:8 - 4 * half]):
                        if d < 3:
                            dve.wait_ge(S["down_added"], 3 * (NF * n + (NF // 2) * (2 - half) - 1) + d + 1)
                        else:
                            dve.wait_ge(S["w_used"], base + 2 * NF + (NF // 2) * (2 - half))
                        nc.vector.scalar_tensor_tensor(x[:, k, :], ps[:, k, :], gate(k), x[:, k, :], ALU.mult, ALU.add).then_inc(S["x_ready"], 1)

            nc.vector.memset(stat[:, 0:100], 0.0).then_inc(S["af_ready"], 2)
            nc.vector.memset(stat[:, 100:150], 0.0).then_inc(S["a_ready"], 2)
            nc.vector.memset(stat[:, 150:200], 0.0).then_inc(S["ada_used"], 1)
            dve.wait_ge(S["basics_loaded"], 48)
            for loaded in x_loaded:
                dve.wait_ge(loaded, 16)
            def rope(unit, cos, sin, rows=slice(0, P), temp=38):
                r = due("rot_ready")
                dve.wait_ge(S["rot_ready"], r)
                t = mem[rows, temp + r % 2, :]
                nc.vector.tensor_tensor(t, ps[rows, 2 + (r - 1) % 2, :], sin, ALU.mult)
                link(nc.vector.tensor_tensor(mem[rows, unit, :], mem[rows, unit, :], cos, ALU.mult))
                nc.vector.tensor_tensor(mem[rows, unit, :], mem[rows, unit, :], t, ALU.add).then_inc(S["roped"], 1)


            def head_inverse(chunks, count):
                dve.wait_ge(S["head_std"], due("head_std"))
                n = 2 * TB * count
                link(nc.vector.reciprocal(head_tok[:, 0:n], head_tok[:, 0:n]))
                wide = chunks.rearrange("p u (c d) -> p (u c) d", d=HD)
                nc.vector.tensor_copy(wide, head_tok[:, 0:n].unsqueeze(2).to_broadcast([P, n, HD])).then_inc(S["head_inv"], 1)


            def attention(l):
                norm_x(lambda k: param("mix_g", KD * l + k))
                nc.vector.memset(rw[:, :, 0:1], 0.0)
                nc.vector.memset(cv[:, :, 0:3], 0.0)
                nc.vector.memset(state[:, :, :], 0.0).then_inc(S["s_out"], 1)
                cos, sin = const("cos", 0, T), const("sin", 0, T)
                first = seen.get("proj_out", 0)
                dve.wait_ge(S["proj_out"], first + 1)
                rope(U_KI, cos, sin)
                for j in range(4):
                    rope(U_QI + j, cos, sin)
                dve.wait_ge(S["wi_ready"], l + 1)
                link(nc.vector.tensor_scalar(stat[:, ST_WI:ST_WI + 32], ps[:, 6, 0:32], float(8 ** -0.5 * HD ** -0.5), None, ALU.mult))
                V = nc.vector
                top = stat[:, ST_TOP:ST_TOP + 8]

                def score(n):
                    return mem[:, 39 + n, 0:(n + 1) * P]

                def best_keys(n, rounds):
                    for r in rounds:
                        link(nc.vector.max(top, score(n)))
                        link(nc.vector.match_replace(score(n), top, score(n), TAKEN))

                for at, (n, h) in enumerate(INDEX_ITEMS):
                    i = due("relu_ready") - 1
                    dve.wait_ge(S["relu_ready"], i + 1)
                    wi = stat[:, ST_WI + 8 * n + h:ST_WI + 8 * n + h + 1]
                    relu = mem[:, 43 + i % 2, 0:(n + 1) * P]
                    if h == 0:
                        nc.vector.tensor_scalar(score(n), relu, wi, None, ALU.mult).then_inc(S["score_added"], 1)
                    else:
                        dve.wait_ge(S["score_added"], i)
                        nc.vector.scalar_tensor_tensor(score(n), relu, wi, score(n), ALU.mult, ALU.add).then_inc(S["score_added"], 1)
                    if h == 7:
                        dve.wait_ge(S["score_added"], i + 1)
                        link(nc.vector.tensor_tensor(score(n)[:, blk(n)], score(n)[:, blk(n)], const("causal_neg"), ALU.add))
                    tile, last = at // INDEX_PER_TILE, at % INDEX_PER_TILE == INDEX_PER_TILE - 1
                    if last and tile >= 2:
                        best_keys(3, range(4 * (tile - 2), 4 * (tile - 1)))
                    if last and tile == 4:
                        head_inverse(mem[:, 33:38, :], 5)
                head0 = seen.get("head_done", 0)
                for s in range(7):
                    if s < 5:
                        gain = param(f"att_k{l}" if s == 0 else f"att_q{l}")
                        dve.wait_ge(S["head_spread"], due("head_spread"))
                        nc.vector.scalar_tensor_tensor(mem[:, U_K + s, :], mem[:, U_K + s, :], gain, ps[:, 4 + s % 2, :], ALU.mult, ALU.mult).then_inc(S["head_done"], 1)
                    if s >= 2:
                        dve.wait_ge(S["head_done"], head0 + s - 1)
                        rope(U_K + s - 2, cos, sin)
                    if s < 4:
                        best_keys(2, range(4 * s, 4 * s + 4))
                    if s == 4:
                        dve.wait_ge(S["proj_out"], first + ATT_TILES + 7)
                        V.tensor_tensor(mem[:, 2:6, :], rw[:, 0:4, 0:T], rw[:, 0:4, 1:T + 1], ALU.subtract)
                        link(V.tensor_tensor(mem[:, 33:36, :], rw[:, 4:7, 0:T], rw[:, 4:7, 1:T + 1], ALU.subtract))
                    if s == 5:
                        for c in range(7):
                            step = mem[:, 2 + c if c < 4 else 33 + c - 4, :]
                            ins = V.scalar_tensor_tensor(rw[:, c, 1:T + 1], step, param(f"mu{l}", c), rw[:, c, 1:T + 1], ALU.mult, ALU.add)
                        ins.then_inc(S["shifted"], 1)
                due("head_done", 5)
                best_keys(1, range(TOPK // 8))
                for n in (3, 2, 1):
                    ins = V.tensor_scalar(score(n), score(n), 0.5 * TAKEN, NEG, ALU.is_gt, ALU.mult)
                link(ins)
                dve.wait_ge(S["shifted"], l + 1)
                dve.wait_ge(S["proj_out"], due("proj_out", ATT_TILES + REC_TILES))
                dve.wait_ge(S["w_used"], BASE[f"rec_in{l}"] + REC_TILES)
                r, k = (rw[:, c:c + 2, 1:T + 1] for c in (0, 2))
                kk, bonus, conv = (core_mem[:, u:u + n, :] for u, n in ((R_KK, 2), (R_SQ, 2), (G_CONV, 6)))
                for c in range(2):
                    V.tensor_scalar(kk[:, c, :], k[:, c, :], param(f"k_k{l}", c), None, ALU.mult)
                    ins = V.tensor_scalar(stat[:, ST_OMKA + c:ST_OMKA + c + 1], param(f"k_a{l}", c), -1.0, 1.0, ALU.mult, ALU.add)
                ins.then_inc(S["kk_in"], 1)

                def meanwhile(i):
                    if i == 2:
                        dve.wait_ge(S["gates_ready"], l + 1)
                        for c in range(2):
                            for n in range(TB):
                                ins = V.tensor_tensor_scan(mem[:, 4 + c, blk(n)], const("ones"), mem[:, c, blk(n)], 0.0, ALU.mult, ALU.add)
                        link(ins)
                        cum = by_block(mem[:, 4:6, :])
                        mid, end, gam = block_columns(ST_CM), block_columns(ST_CE), block_columns(ST_GAMMA)
                        V.tensor_copy(mid, cum[:, :, :, HD - 1])
                        link(V.tensor_copy(end, cum[:, :, :, P - 1]))
                        link(V.tensor_tensor(gam, end, mid, ALU.subtract))
                        V.tensor_tensor(gam[:, :, 0:TB - 1], gam[:, :, 0:TB - 1], mid[:, :, 1:TB], ALU.add)
                        link(V.tensor_tensor(cum, cum, mid.unsqueeze(3).to_broadcast([P, 2, TB, P]), ALU.subtract))
                        V.tensor_tensor(mem[:, 0:2, :], mem[:, 4:6, :], mem[:, 0:2, :], ALU.subtract).then_inc(S["decay_in"], 1)
                    if i == 6:
                        head_inverse(core_mem[:, R_SQ:R_SQ + 2, :], 2)
                    if i == 8:
                        dve.wait_ge(S["head_spread"], due("head_spread"))
                        V.tensor_tensor(kk, kk, ps[:, 0:2, :], ALU.mult).then_inc(S["head_done"], 1)
                    if i == 9:
                        dve.wait_ge(S["head_done"], due("head_done"))
                        dve.wait_ge(S["decay_ready"], l + 1)
                        link(V.tensor_tensor(mem[:, 46:48, :], kk, mem[:, 35:37, :], ALU.mult))
                    if i == 10:
                        link(V.tensor_tensor(kk, kk, mem[:, 2:4, :], ALU.mult))
                    if i == 11:
                        for c in range(2):
                            ins = V.tensor_scalar(mem[:, 2 + c, :], mem[:, 2 + c, :], param(f"k_a{l}", c), stat[:, ST_OMKA + c:ST_OMKA + c + 1], ALU.mult, ALU.add)
                        link(ins)
                    if i == 12:
                        link(V.tensor_tensor(k, k, mem[:, 2:4, :], ALU.mult))
                    if i == 13:
                        for c in range(2):
                            ins = V.scalar_tensor_tensor(bonus[:, c, :], r[:, c, :], param(f"r_k{l}", c), k[:, c, :], ALU.mult, ALU.mult)
                        ins.then_inc(S["bonus_in"], 1)
                    if i == 14:
                        dve.wait_ge(S["bonus_in"], l + 1)
                        V.tensor_tensor(k, k, mem[:, 37:39, :], ALU.mult)
                    if i == 15:
                        V.tensor_tensor(r, r, mem[:, 33:35, :], ALU.mult)
                    if 16 <= i < 28:
                        tap, pair = (i - 16) // 3, (i - 16) % 3
                        for c in range(2 * pair, 2 * pair + 2):
                            w = param(f"conv{l}", 6 * tap + c)
                            if tap == 0:
                                ins = V.tensor_scalar(conv[:, c, :], cv[:, c, 0:T], w, None, ALU.mult)
                            else:
                                ins = V.scalar_tensor_tensor(conv[:, c, :], cv[:, c, tap:tap + T], w, conv[:, c, :], ALU.mult, ALU.add)
                        if i == 27:
                            ins.then_inc(S["conv_ready"], 1)
                        elif pair == 2:
                            link(ins)
                    s = mem[ROW_A:ROW_A + 4, U_MISC, :]
                    if i == 28:
                        link(V.tensor_scalar(s, s, param(f"dt{l}")[ROW_A:ROW_A + 4, :], None, ALU.add))
                    if i == 29:
                        link(V.scalar_tensor_tensor(soft, s, -1.0, s, ALU.mult, ALU.min))
                    if i == 30:
                        V.tensor_scalar(s, s, 0.0, None, ALU.max).then_inc(S["sp_in"], 1)

                i0 = seen.get("items", 0)
                for i in range(len(ITEMS) + 1):
                    meanwhile(i)
                    if i % 8 == 2 and i > 2:
                        outputs(i0 + i - 2)
                    if i == len(ITEMS):
                        break
                    n = ITEMS[i][0]
                    w = (n + 1) * P
                    dve.wait_ge(S["s_ready"], i0 + i + 1)
                    if i0 + i >= 2:
                        dve.wait_ge(S["p_turned"], i0 + i - 1)
                    p = core_mem[:, S_P + i % 2, 0:w]
                    mask = const("causal_neg") if n == 0 else mem[:, 39 + n, 0:w]
                    nc.vector.scalar_tensor_tensor(p, ps[:, 2 + i % 2, 0:w], HD ** -0.5, mask, ALU.mult, ALU.add).then_inc(S["score_taken"], 1)
                    dve.wait_ge(S["score_taken"], i0 + i + 1)
                    top1 = stat[:, ST_MAX + i:ST_MAX + i + 1]
                    link(nc.vector.reduce_max(top1, p, AX_X))
                    nc.vector.tensor_scalar(top1, top1, -1.0, None, ALU.mult).then_inc(S["max_ready"], 1)
                outputs(i0 + len(ITEMS))
                due("items", len(ITEMS))


            def outputs(items):
                g = (items // 8 - 1) % TB
                dve.wait_ge(S["pv_done"], items)
                inv = stat[:, ST_INV:ST_INV + 8]
                link(nc.vector.reciprocal(inv, stat[:, ST_SUM + 8 * g:ST_SUM + 8 * g + 8]))
                o = lambda ap: ap.rearrange("p (h d) -> p h d", d=HD)
                if items > 8:
                    dve.wait_ge(S["ot_ready"], items // 8 - 1)
                nc.vector.tensor_tensor(o(core_mem[:, S_OUT, :]), o(ps[:, 6, :]), inv.unsqueeze(2).to_broadcast([P, 8, HD]), ALU.mult).then_inc(S["o_taken"], 1)


            def block_columns(at):
                return stat[:, at:at + 2 * TB].rearrange("p (c n) -> p c n", c=2)


            def recurrences(l):
                dve.wait_ge(S["y_att_out"], TB * (l + 1))
                V = nc.vector
                kk, gate, v = core_mem[:, R_KK:R_KK + 2, :], core_mem[:, R_SQ:R_SQ + 2, :], rw[:, 4:6, 1:T + 1]
                V.scalar_tensor_tensor(mem[:, 7:9, :], kk, -1.0, mem[:, 37:39, :], ALU.mult, ALU.mult).then_inc(S["rwkv_ready"], 1)
                if l > 0:
                    dve.wait_ge(S["v_gate"], 1)
                    dve.wait_ge(S["vf_moved"], 32)
                    link(V.tensor_tensor(mem[:, 9:11, :], mem[:, 9:11, :], v, ALU.subtract))
                    link(V.tensor_tensor(mem[:, 9:11, :], mem[:, 9:11, :], gate, ALU.mult))
                    link(V.tensor_tensor(v, v, mem[:, 9:11, :], ALU.add))
                dve.wait_ge(S["bonus_sum"], l + 1)
                V.tensor_tensor(mem[:, 9:11, :], ps[:, 0:2, :], v, ALU.mult).then_inc(S["bonus_taken"], 1)
                s, g = (mem[ROW_A:ROW_A + 4, u, :] for u in (U_MISC, 6))
                dve.wait_ge(S["sp_ln"], l + 1)
                link(V.tensor_tensor(s, s, soft, ALU.add))
                link(V.tensor_scalar(s, s, stat[ROW_A:ROW_A + 4, ST_EA:ST_EA + 1], -1.0, ALU.mult, ALU.mult))
                for n in range(TB):
                    ins = V.tensor_tensor_scan(g[:, blk(n)], const("ones")[ROW_A:ROW_A + 4, :], s[:, blk(n)], 0.0, ALU.mult, ALU.add)
                ins.then_inc(S["g_ready"], 1)
                for n, u in enumerate((0, 1, 4, 5, 2, 3) if l == 0 else (), 1):
                    dve.wait_ge(S["turned"], n)
                    V.tensor_copy(mem[:, u, :], ps[:, n % 2, :]).then_inc(S["turned_out"], 1)
                dve.wait_ge(S["sp_in"], l + 1)
                head_inverse(mem[:, 39:43, :], 4)
                dve.wait_ge(S["head_spread"], due("head_spread"))
                V.scalar_tensor_tensor(mem[:, 33:35, :], mem[:, 33:35, :], HD ** -0.5, ps[:, 2:4, :], ALU.mult, ALU.mult)
                V.tensor_tensor(mem[:, 35:37, :], mem[:, 35:37, :], ps[:, 4:6, :], ALU.mult).then_inc(S["head_done"], 1)
                dve.wait_ge(S["head_done"], due("head_done"))
                dve.wait_ge(S["g_turned"], l + 1)
                V.tensor_scalar(stat[:, ST_GNEG:ST_GNEG + 16], ps[:, 0, 0:16], -1.0, None, ALU.mult).then_inc(S["g_taken"], 1)
                dve.wait_ge(S["g_taken"], l + 1)
                dve.wait_ge(S["spread_ready"], 6 * l + 1)
                V.tensor_copy(block_columns(ST_GLAST), by_block(ps[:, 2:4, :])[:, :, :, P - 1]).then_inc(S["spread_taken"], 1)
                dve.wait_ge(S["spread_ready"], 6 * l + 2)
                V.tensor_tensor(mem[:, 39:41, :], mem[:, 35:37, :], ps[:, 0:2, :], ALU.mult)
                V.tensor_tensor(mem[:, 37:39, :], mem[:, 37:39, :], ps[:, 0:2, :], ALU.mult).then_inc(S["spread_taken"], 1)
                dve.wait_ge(S["eg_ready"], 2 * l + 2)
                V.tensor_copy(block_columns(ST_EGL), by_block(mem[:, 41:43, :])[:, :, :, P - 1])
                V.tensor_tensor(mem[:, 24:26, :], mem[:, 35:37, :], mem[:, 24:26, :], ALU.mult).then_inc(S["kd_ready"], 1)
                for h in range(4):
                    dve.wait_ge(S["spread_ready"], 6 * l + 3 + h)
                    for n in range(TB):
                        at = ST_GNEG + 4 * n + h
                        ins = V.scalar_tensor_tensor(mem[:, 20 + n, blk(2 * (h % 2) + h // 2)], ps[:, 4 + h, blk(n)], stat[:, at:at + 1], const("decay_neg"), ALU.add, ALU.add)
                ins.then_inc(S["spread_taken"], 1)
                dve.wait_ge(S["turned"], 10 * (l + 1))
                V.tensor_tensor(mem[:, 37:39, :], mem[:, 33:35, :], mem[:, 41:43, :], ALU.mult)
                V.scalar_tensor_tensor(mem[:, 24:26, :], mem[:, 39:41, :], -1.0, mem[:, 41:43, :], ALU.mult, ALU.mult).then_inc(S["gdn_ready"], 1)
                dve.wait_ge(S["dt_ready"], l + 1)
                dve.wait_ge(S["turned_out"], 10 * (l + 1))
                for n in range(TB + 1):
                    core_step(l, n)
                post(l)


            def core_step(l, n):
                V = nc.vector
                b = TB * l + n
                cm = core_mem
                half = slice(0, HALF), slice(HALF, T)

                def strict_part(lev, g):
                    V.tensor_tensor(heads(cm[:, C_N + g, :]), heads(cm[:, C_L + g, :]), over_heads(const("levels", lev * P)), ALU.mult).then_inc(S["n_ready"], 1)

                def level(lev, g):
                    e = 2 * (N_LEVELS * b + lev) + g
                    dve.wait_ge(S["t1_ready"], e + 1)
                    dve.wait_ge(S["n_ready"], e + 1)
                    inv, inv_t = cm[:, C_INV + g, :], cm[:, inv_t_unit(n, g), :]
                    if lev == 0:
                        V.tensor_tensor(heads(inv), heads(ps[:, 2 + g, :]), over_heads(const("ident")), ALU.add)
                        V.tensor_tensor(heads(inv_t), heads(cm[:, C_N + g, :]), over_heads(const("ident")), ALU.add).then_inc(S["inv_ready"], 1)
                        dve.wait_ge(S["inv_ready"], e + 1)
                        strict_part(1, g)
                        return
                    if lev < N_LEVELS - 1:
                        strict_part(lev + 1, g)
                    dve.wait_ge(S["dx_ready"], 2 * ((N_LEVELS - 1) * b + lev - 1) + g + 1)
                    if lev < N_LEVELS - 1:
                        V.tensor_tensor(evens(inv, lev), evens(inv, lev), compact(ps[:, 4 + g, half[0]], lev), ALU.add)
                    V.tensor_tensor(odds(inv_t, lev), odds(inv_t, lev), compact(ps[:, 4 + g, half[1]], lev), ALU.add).then_inc(S["inv_ready"], 1)

                def a_grams():
                    pair = lambda ap: ap.rearrange("p (h t) -> p h t", h=2)
                    both = lambda mask: const(mask).unsqueeze(1).to_broadcast([P, 2, P])
                    decay = mem[:, 20 + n - 1, :]
                    for g in range(4):
                        dve.wait_ge(S["a_gram_ready"], 4 * (b - 1) + g + 1)
                        out, src = cm[:, C_A + g, :], ps[:, (0, 1, 6, 7)[g], :]
                        V.tensor_tensor(pair(out[:, half[0]]), pair(src[:, half[0]]), both("strict" if g < 2 else "incl"), ALU.mult)
                        if g < 2:
                            ins = V.tensor_tensor(pair(out[:, half[1]]), pair(src[:, half[1]]), both("incl"), ALU.mult)
                        else:
                            ins = V.tensor_tensor(out[:, half[1]], src[:, half[1]], decay[:, half[g - 2]], ALU.mult)
                        ins.then_inc(S["a_gram_out"], 1)

                def next_state():
                    dve.wait_ge(S["s_next"], (TB - 1) * l + n)
                    dve.wait_ge(S["y_ready"], b)
                    link(V.tensor_tensor(state[:, 0:2, :], state[:, 0:2, :], ps[:, 1, 0:P].rearrange("p (c d) -> p c d", c=2), ALU.add))
                    for c in range(2):
                        at = TB * c + n - 1
                        V.tensor_scalar(state[:, c, :], state[:, c, :], stat[:, ST_GAMMA + at:ST_GAMMA + at + 1], None, ALU.mult)
                        ins = V.scalar_tensor_tensor(state[:, 2 + c, :], state[:, 2 + c, :], stat[:, ST_EGL + at:ST_EGL + at + 1],
                                                     ps[:, 1, P + HD * c:P + HD * c + HD], ALU.mult, ALU.add)
                    ins.then_inc(S["s_out"], 1)

                if n < TB:
                    decay = mem[:, 20 + n, :]
                    for g in range(2):
                        dve.wait_ge(S["gram_ready"], 2 * b + g + 1)
                        V.tensor_copy(cm[:, C_L + g, half[0]], ps[:, g, half[0]])
                        V.scalar_tensor_tensor(cm[:, C_L + g, half[1]], ps[:, g, half[1]], -1.0, decay[:, half[g]], ALU.mult, ALU.mult).then_inc(S["gram_taken"], 1)
                    dve.wait_ge(S["gram_taken"], 2 * b + 2)
                    for g in range(2):
                        strict_part(0, g)
                for lev in range(N_LEVELS):
                    if n < TB:
                        for g in range(2):
                            level(lev, g)
                    if n and lev == 0:
                        a_grams()
                    if 0 < n < TB and lev == 5:
                        next_state()


            def post(l):
                V = nc.vector
                y, o = rw[:, 0:2, 1:T + 1], mem[:, 37:39, :]
                attended = lambda k, slot: V.tensor_copy(slot, mem[:, U_Y + k, :])
                dve.wait_ge(S["mean_ready"], l + 1)
                V.scalar_tensor_tensor(y, ps[:, 0:2, :], -1.0 / HD, y, ALU.mult, ALU.add).then_inc(S["centred"], 1)
                split_h((0, 1), attended)
                head_inverse(mem[:, 35:37, :], 2)
                split_h((2, 3), attended)
                dve.wait_ge(S["head_spread"], due("head_spread"))
                V.scalar_tensor_tensor(o, o, param(f"o_norm{l}"), ps[:, 4:6, :], ALU.mult, ALU.mult).then_inc(S["head_done"], 1)
                head_inverse(mem[:, 33:35, :], 2)
                dve.wait_ge(S["head_spread"], due("head_spread"))
                V.tensor_tensor(y, y, ps[:, 2:4, :], ALU.mult).then_inc(S["head_done"], 1)
                dve.wait_ge(S["head_done"], due("head_done", 2))
                for c in range(2):
                    ins = V.tensor_scalar(y[:, c, :], y[:, c, :], param(f"gn_w{l}", c), param(f"gn_b{l}", c), ALU.mult, ALU.add)
                link(ins)
                link(V.tensor_tensor(y, y, mem[:, 9:11, :], ALU.add))

                def make(k, slot):
                    if k < 6:
                        return V.tensor_tensor(slot, y[:, k - 4, :], mem[:, 43 + k - 4, :], ALU.mult)
                    return V.tensor_tensor(slot, o[:, k - 6, :], mem[:, U_Z + k - 6, :], ALU.mult)

                split_h(range(4, KD), make)
                base = BASE[f"mix_out{l}"]
                for k in range(KD):
                    dve.wait_ge(S["w_used"], base + k + 1)
                    V.tensor_tensor(x[:, k, :], x[:, k, :], ps[:, (k - 1) % KD, :], ALU.add).then_inc(S["x_ready"], 1)


            def modulate(layer, part, gain, which=0, slot=0):
                link(nc.vector.scalar_tensor_tensor(gmod[:, slot, :], ada_cols(layer, part + 1, which), 1.0, gain, ALU.add, ALU.mult))


            def add_gated(base, layer):
                for k in range(KD):
                    dve.wait_ge(S["w_used"], base + k + 1)
                    nc.vector.scalar_tensor_tensor(x[:, k, :], ps[:, (k - 1) % KD, :], ada_col(layer, 2, k), x[:, k, :], ALU.mult, ALU.add).then_inc(S["x_ready"], 1)


            def mla():
                V = nc.vector
                modulate(0, 0, param("mix_g", 2 * KD, KD))
                modulate(0, 0, param("mix_g", 2 * KD, KD), 1, 1)
                norm_x(lambda k: gmod[:, 0, k:k + 1], lambda k: ada_col(0, 0, k))
                dve.wait_ge(S["ctx_std"], 1)
                std = mem2[:, CTX_STD, 0:CTX]
                link(V.reciprocal(std, std))
                for k in range(KD):
                    ins = V.scalar_tensor_tensor(ctx_x[:, k, :], ctx_x[:, k, :], gmod[:, 1, k:k + 1], std, ALU.mult, ALU.mult)
                link(ins)
                for k in range(KD):
                    ins = V.tensor_scalar(ctx_x[:, k, :], ctx_x[:, k, :], ada_col(0, 0, k, 1), None, ALU.add)
                ins.then_inc(S["ctx_f"], 1)
                dve.wait_ge(S["ctx_hi"], 1)
                V.tensor_tensor(hc_lo[:, :, :], ctx_x, hc_hi[:, :, :].bitcast(F32), ALU.subtract).then_inc(S["ctx_ready"], 1)
                dve.wait_ge(S["ctx_ready"], 1)
                dve.wait_ge(S["proj_out"], due("proj_out", 6))
                dve.wait_ge(S["ctx_out"], 3)
                dve.wait_ge(S["lat_std"], 1)
                V.reciprocal(head_tok[:, 0:TB + KB], head_tok[:, 0:TB + KB]).then_inc(S["lat_inv"], 1)
                dve.wait_ge(S["lat_spread"], 1)
                for w, (factor, lat, hi, lo, gain, width) in enumerate(((ps[:, 4, :], cq, cq_hi, cq_lo, "mla_qn", 3),
                                                                        (psf[:, 5 * T:5 * T + TK], ckv, ckv_hi, ckv_lo, "mla_kvn", 2))):
                    for c in range(width):
                        ins = V.scalar_tensor_tensor(lat[:, c, :], lat[:, c, :], param(gain, c), factor, ALU.mult, ALU.mult)
                    ins.then_inc(S["lat_f"], 1)
                    dve.wait_ge(S["lat_f"], w + 1)
                    dve.wait_ge(S["lat_hi"], w + 1)
                    V.tensor_tensor(lo[:, :, :], lat, hi[:, :, :].bitcast(F32), ALU.subtract).then_inc(S["lat_ready"], 1)
                base = BASE["mla_in"]
                V.memset(z_conv[:, 0:1], 0.0)
                link(V.memset(z_conv[:, T + 1:T + 2], 0.0))
                for j in range(4):
                    y = mem2[:, Y_CONV + j, :]
                    dve.wait_ge(S["c_out"], j + 1)
                    dve.wait_ge(S["w_used"], base + 8 + 3 * j)
                    V.tensor_tensor(z_conv[:, 1:T + 1], mem2[:, j % 2, :], ps[:, 1, :], ALU.mult).then_inc(S["u_taken"], 1)
                    dve.wait_ge(S["u_taken"], j + 1)
                    link(V.tensor_scalar(y, z_conv[:, 0:T], param("short_conv", j), None, ALU.mult))
                    for tap in (1, 2):
                        link(V.scalar_tensor_tensor(y, z_conv[:, tap:tap + T], param("short_conv", 4 * tap + j), y, ALU.mult, ALU.add))
                    dve.wait_ge(S["w_used"], base + 9 + 3 * j)
                    V.tensor_tensor(y, y, ps[:, 2, :], ALU.mult).then_inc(S["conv_taken"], 1)
                dve.wait_ge(S["w_used"], base + 18)
                V.tensor_copy(kmla[PE_ROWS, :, :], kpe[PE_ROWS, :].unsqueeze(1).to_broadcast([32, 8, TK])).then_inc(S["kpe_ready"], 1)
                dve.wait_ge(S["consts2_loaded"], 16)

                def rotate(i):
                    x_pe = mem2[PE_ROWS, Q_MLA + i, :] if i < 8 else kmla[PE_ROWS, i - 8, 0:T]
                    t = mem2[PE_ROWS, i % 2, :]
                    dve.wait_ge(S["rot2_ready"], i + 1)
                    V.tensor_tensor(t, ps[PE_ROWS, 7, :], const2("sin2", T)[PE_ROWS, :], ALU.mult)
                    link(V.tensor_tensor(x_pe, x_pe, const2("cos2", T)[PE_ROWS, :], ALU.mult))
                    V.tensor_tensor(x_pe, x_pe, t, ALU.add).then_inc(S["rot2_done"], 1)

                for i in range(16):
                    head = mem2[0:QKD, Q_MLA + i, :] if i < 8 else kmla[0:QKD, i - 8, :]
                    dve.wait_ge(S["qk_std"], i + 1)
                    V.reciprocal(qk_tok(i), qk_tok(i)).then_inc(S["qk_inv"], 1)
                    if i:
                        rotate(i - 1)
                    dve.wait_ge(S["qk_spread"], i + 1)
                    V.scalar_tensor_tensor(head, head, param("q_gain" if i < 8 else "k_gain")[0:QKD, :], psf[0:QKD, 4 * T:4 * T + qk_width(i)],
                                           ALU.mult, ALU.mult).then_inc(S["qk_done"], 1)
                dve.wait_ge(S["qk_done"], 16)
                rotate(15)
                dve.wait_ge(S["rot2_done"], 16)
                i0 = seen["items"]
                scale = float(QKD ** -0.5)

                def turn_out(i):
                    dve.wait_ge(S["p_turned"], i0 + i + 1)
                    if i >= 2:
                        dve.wait_ge(S["pv_done"], i0 + i - 1)
                    V.tensor_copy(wide[i % 2], psf[:, 4 * T:4 * T + TK]).then_inc(S["pt_out"], 1)

                for i in range(33):
                    if i % 8 == 2 and i > 2:
                        mla_outputs(i0 + i - 2)
                    if i < 32:
                        at = 2 * (i % 2) * T
                        top1 = stat[:, ST_MAX + i:ST_MAX + i + 1]
                        dve.wait_ge(S["s_ready"], i0 + i + 1)
                        link(V.reduce_max(top1, psf[:, at:at + TK], AX_X))
                        V.tensor_scalar(top1, top1, -scale, None, ALU.mult).then_inc(S["max_ready"], 1)
                    if i:
                        turn_out(i - 1)
                mla_outputs(i0 + 32)
                due("items", 32)
                dve.wait_ge(S["y_att_out"], 3 * TB)
                dve.wait_ge(S["conv_taken"], 4)
                split_h(range(KD), lambda k, slot: V.tensor_copy(slot, mem2[:, (Y_MLA + k) if k < 4 else (Y_CONV + k - 4), :]))
                add_gated(BASE["mla_out"], 0)


            def mla_outputs(items):
                g = (items // 8 - 1) % TB
                dve.wait_ge(S["pv_done"], items)
                inv = stat[:, ST_INV:ST_INV + 8]
                link(nc.vector.reciprocal(inv, stat[:, ST_SUM + 8 * g:ST_SUM + 8 * g + 8]))
                o = lambda ap: ap.rearrange("p (h d) -> p h d", d=HD)
                dve.wait_ge(S["ot_ready"], items // 8 - 1)
                nc.vector.tensor_tensor(o(mem2[:, O_MLA, :]), o(ps[:, 6, :]), inv.unsqueeze(2).to_broadcast([P, 8, HD]), ALU.mult).then_inc(S["o_taken"], 1)


            def fourier():
                V = nc.vector
                modulate(1, 0, param("mix_g", 3 * KD, KD))
                norm_x(lambda k: gmod[:, 0, k:k + 1], lambda k: ada_col(1, 0, k))
                for i in range(16):
                    dve.wait_ge(S["g_hi_ready"], i + 1)
                    V.tensor_tensor(g_lo[:, i, :], ps[:, i % 4, :], g_hi[:, i, :].bitcast(F32), ALU.subtract).then_inc(S["g_split"], 1)
                dve.wait_ge(S["w_used"], BASE["dft_time"] + 4)
                split_h(FROM_LAST, lambda k, slot: V.tensor_copy(slot, ps[:, k, :]))
                add_gated(BASE["fourier_out"], 1)
            for name in run:
                l = int(name[-1]) if name[-1].isdigit() else None
                if name.startswith("ffn") and l < 4:
                    ffn(l, lambda k: param("ffn_g", KD * l + k), None, lambda k: 0.5)
                if name == "ffn0":
                    dve.wait_ge(S["consts_loaded"], 64)
                if name.startswith("rec_in"):
                    attention(l)
                if name.startswith("mix_out"):
                    recurrences(l)
                if name == "mla_out":
                    mla()
                if name.startswith("ffn") and l >= 4:
                    modulate(l - 4, 3, param("ffn_g", KD * l, KD))
                    ffn(l, lambda k: gmod[:, 0, k:k + 1], lambda k: ada_col(l - 4, 3, k), lambda k: ada_col(l - 4, 5, k))
                if name == "fourier_out":
                    fourier()

        @block.tensor
        def _(pe):
            seen = {}

            def due(name, n=1):
                seen[name] = seen.get(name, 0) + n
                return seen[name]

            def products(bank, slot, cols, hi, lo, first, last, w_first=True):
                wh, wl = w_hi[:, slot, cols:cols + P], w_lo[:, slot, cols:cols + P]
                nc.tensor.matmul(bank, wh, hi, start=first, stop=False, skip_group_check=True)
                nc.tensor.matmul(bank, wh, lo, start=False, stop=False, skip_group_check=True)
                return nc.tensor.matmul(bank, wl, hi, start=False, stop=last, skip_group_check=True)

            def linear_tile(bank, t, i=None, step=RING):
                pe.wait_ge(S["w_lo_ready"], t + 1 if i is None else step * i + (t + 1))
                for k in range(KD):
                    ins = products(bank, t % RING, k * P, h_hi[:, k, :], h_lo[:, k, :], k == 0, k == KD - 1)
                ins.then_inc(S["w_used"], 1)

            def first_tiles(t, banks=(0, 1), order=range(KD)):
                pe.wait_ge(S["w_lo_ready"], t + 2)
                for n, k in enumerate(order):
                    pe.wait_ge(S["h_hi_ready"], due("h_ready"))
                    for r in range(2):
                        block, slot = slice(k * P, (k + 1) * P), (t + r) % RING
                        nc.tensor.matmul(ps[:, banks[r], :], w_hi[:, slot, block], h_hi[:, k, :], start=(n == 0), stop=False, skip_group_check=True)
                        nc.tensor.matmul(ps[:, banks[r], :], w_lo[:, slot, block], h_hi[:, k, :], start=False, stop=False, skip_group_check=True)
                    pe.wait_ge(S["h_ready"], seen["h_ready"])
                    for r in range(2):
                        block, slot = slice(k * P, (k + 1) * P), (t + r) % RING
                        ins = nc.tensor.matmul(ps[:, banks[r], :], w_hi[:, slot, block], h_lo[:, k, :], start=False, stop=(n == KD - 1), skip_group_check=True)
                        if n == KD - 1:
                            ins.then_inc(S["w_used"], 1)

            def sum_chunk(n):
                pe.wait_ge(S["sq_ready"], due("sq_ready"))
                for j in range(TB):
                    ins = nc.tensor.matmul(ps[:, 7, j:j + 1], squares[n % len(squares)][:, j * P:(j + 1) * P], const("ones", 0, 1),
                                           start=(n == 0 and j == 0), stop=(n == KD - 1), skip_group_check=True)
                ins.then_inc(S["ss_ready"], 1)
                seen["early"] = n + 1

            def sum_squares():
                for n in range(seen.get("early", 0), KD):
                    sum_chunk(n)
                seen["early"] = 0
                pe.wait_ge(S["rtok_ready"], due("rtok_ready"))
                for j in range(TB):
                    ins = nc.tensor.matmul(ps[:, 7, j * P:(j + 1) * P], rtok[:, j:j + 1].to_broadcast([P, P]), const("ident"), start=True, stop=True)
                ins.then_inc(S["rstd_ready"], 1)

            def ffn(n):
                base = BASE[f"ffn{n}"]
                sum_squares()

                def up_pair(i, j):
                    pe.wait_ge(S["af_ready"], NF * n + 2 * i + (j + 1))
                    linear_tile(ps[:, 2 * j, :], base + 2 * j, i)
                    linear_tile(ps[:, 2 * j + 1, :], base + 2 * j + 1, i)

                pe.wait_ge(S["af_ready"], NF * n + 1)
                first_tiles(base)
                up_pair(0, 1)
                with pe.Fori(1, NF // 2) as i:
                    for j in range(2):
                        up_pair(i, j)
                down = base + 2 * NF

                def down_tile(half, pair, i=None):
                    t = down + (1 - half) * (NF // 2) + pair
                    turn = 0 if i is None else RING * i
                    pe.wait_ge(S["w_lo_ready"], turn + (t + 1))
                    if half:
                        pe.wait_ge(S["a_ready"], 2 * turn + (NF * n + 2 * pair + 4))
                    for d, c in enumerate(FFN_ORDER[4 - 4 * half:8 - 4 * half]):
                        for f in range(2):
                            at = 2 * turn + (2 * pair + f)
                            ins = products(ps[:, c, :], t % RING, f * 4 * P + c % 4 * P, a_hi[:, at, :], a_lo[:, at, :],
                                           i is None and pair + f == 0, False)
                        ins.then_inc(S["down_added"] if d < 3 else S["w_used"], 1)

                for half in (1, 0):
                    if half == 0:
                        pe.wait_ge(S["af_ready"], NF * n + NF + 2)
                    for pair in range(LONE_PAIRS):
                        down_tile(half, pair)
                    if half == 0 and n < 2 * DEPTH + 1:
                        for c in range(KD // 2):
                            sum_chunk(c)
                    with pe.Fori(0, (NF // 2 - LONE_PAIRS) // RING) as i:
                        for r in range(RING):
                            down_tile(half, LONE_PAIRS + r, i)

            pe.wait_ge(S["basics_loaded"], 48)
            def head_sums(chunks, bank, column=0):
                for c, chunk in enumerate(chunks):
                    for n in range(TB):
                        at = 2 * TB * (column + c) + 2 * n
                        ins = nc.tensor.matmul(ps[:, bank, at:at + 2], chunk[:, blk(n)], const("ones_head")[:, 0:P:HD], start=True, stop=True)
                return ins


            def head_spread(chunk, bank):
                for n in range(TB):
                    ins = nc.tensor.matmul(ps[:, bank, blk(n)], chunk[:, blk(n)], const("ident"), start=True, stop=True)
                return ins


            def head_norms(chunks, sums, banks):
                pe.wait_ge(S["head_sq"], due("head_sq"))
                head_sums(chunks, sums).then_inc(S["head_sum"], 1)
                pe.wait_ge(S["head_inv"], due("head_inv"))
                for chunk, bank in zip(chunks, banks):
                    ins = head_spread(chunk, bank)
                ins.then_inc(S["head_spread"], 1)


            def mem_units(*units):
                return [mem[:, u, :] for u in units]


            def attention(l):
                base = BASE[f"att_in{l}"]
                first = seen.get("proj_out", 0)
                rot0 = seen.get("rot", 0)
                sum_squares()

                def rot(unit):
                    r = due("rot") - 1
                    if r - rot0 >= 2:
                        pe.wait_ge(S["roped"], r - 1)
                    nc.tensor.matmul(ps[:, 2 + r % 2, :], const("rot"), mem[:, unit, :], start=True, stop=True).then_inc(S["rot_ready"], 1)

                def head_sum(s):
                    pe.wait_ge(S["head_sq"], due("head_sq"))
                    return head_sums(mem_units(33 + s), 4, s)

                first_tiles(base)
                for m in range(2, ATT_TILES):
                    pe.wait_ge(S["proj_out"], first + m - 1)
                    linear_tile(ps[:, m % 2, :], base + m)
                    if m == 2:
                        rot(U_KI)
                    if m == 3:
                        for n in range(TB):
                            ins = nc.tensor.transpose(ps[:, 6, 8 * n:8 * n + 8], mem[ROW_WI:ROW_WI + 8, U_MISC, blk(n)], const("ident")[0:8, 0:8])
                        ins.then_inc(S["wi_ready"], 1)
                    if 4 <= m < 8:
                        rot(U_QI + m - 4)
                    if 8 <= m < 12:
                        head_sum(m - 8)
                due("proj_out", ATT_TILES)
                base = BASE[f"rec_in{l}"]
                first = seen["proj_out"]
                head0 = seen.get("head_done", 0)
                for m in range(REC_TILES):
                    pe.wait_ge(S["proj_out"], first + m - 1)
                    linear_tile(ps[:, m % 2, :], base + m)
                    if m == 0:
                        pe.wait_ge(S["proj_out"], first)
                        for n in range(TB):
                            ins = nc.tensor.transpose(ps[:, 7, blk(n)], mem[:, U_V, blk(n)], const("ident"))
                        ins.then_inc(S["v_ready"], 1)
                        pe.wait_ge(S["roped"], due("roped", 5))
                    for n, h in INDEX_ITEMS[INDEX_PER_TILE * m:INDEX_PER_TILE * (m + 1)]:
                        i = due("index") - 1
                        if i >= 2:
                            pe.wait_ge(S["relu_ready"], i - 1)
                        rows = slice(HD * (h % 2), HD * (h % 2) + HD)
                        nc.tensor.matmul(ps[:, 2 + i % 2, 0:(n + 1) * P], mem[rows, U_QI + h // 2, blk(n)], mem[rows, U_KI, 0:(n + 1) * P],
                                         start=True, stop=True).then_inc(S["index_ready"], 1)
                    if m == 0:
                        head_sum(4).then_inc(S["head_sum"], 1)
                    if m == 6:
                        pe.wait_ge(S["head_inv"], due("head_inv"))
                    if 6 <= m < 11:
                        if m >= 8:
                            pe.wait_ge(S["head_done"], head0 + m - 7)
                        head_spread(mem[:, 33 + m - 6, :], 4 + m % 2).then_inc(S["head_spread"], 1)
                    if m == 8:
                        pe.wait_ge(S["relu_ready"], len(INDEX_ITEMS) * (l + 1))
                    if 8 <= m < 13:
                        pe.wait_ge(S["head_done"], head0 + m - 7)
                        rot(U_K + m - 8)
                due("head_done", 5)
                due("proj_out", REC_TILES)
                pe.wait_ge(S["roped"], due("roped", 5))
                pe.wait_ge(S["lora_in"], l + 1)
                pe.wait_ge(S["v_out"], l + 1)
                lg = rw[:, 6, 1:T + 1]
                for bank, rows in ((2, slice(0, 32)), (4, slice(32, 64)), (6, slice(64, 128))):
                    for c in range(2):
                        ins = nc.tensor.matmul(ps[:, bank + c, :], lora[rows, l, blk(c)], lg[rows, :], start=True, stop=True)
                ins.then_inc(S["lora_ready"], 1)
                pe.wait_ge(S["gates_ready"], l + 1)

                def meanwhile(i):
                    squares_of_keys = [core_mem[:, R_SQ + c, :] for c in range(2)]
                    if i == 2:
                        pe.wait_ge(S["head_sq"], due("head_sq"))
                        head_sums(squares_of_keys, 0).then_inc(S["head_sum"], 1)
                    if i == 7:
                        pe.wait_ge(S["head_inv"], due("head_inv"))
                        for c in range(2):
                            ins = head_spread(squares_of_keys[c], c)
                        ins.then_inc(S["head_spread"], 1)
                    if i == 16:
                        pe.wait_ge(S["head_done"], due("head_done"))
                        pe.wait_ge(S["bonus_in"], l + 1)
                        for c in range(2):
                            ins = nc.tensor.matmul(ps[:, c, :], const("ones_head"), squares_of_keys[c], start=True, stop=True)
                        ins.then_inc(S["bonus_sum"], 1)

                i0 = seen.get("items", 0)
                pe.wait_ge(S["v_out"], l + 1)
                for i in range(len(ITEMS) + 2):
                    meanwhile(i)
                    if i < len(ITEMS):
                        n, c, hh = ITEMS[i]
                        rows = slice(HD * hh, HD * hh + HD)
                        if i >= 2:
                            pe.wait_ge(S["score_taken"], i0 + i - 1)
                        nc.tensor.matmul(ps[:, 2 + i % 2, 0:(n + 1) * P], mem[rows, U_Q + c, blk(n)], mem[rows, U_K, 0:(n + 1) * P],
                                         start=True, stop=True).then_inc(S["s_ready"], 1)
                    if 1 <= i <= len(ITEMS):
                        n = ITEMS[i - 1][0]
                        pe.wait_ge(S["p_ready"], i0 + i)
                        if i >= 3:
                            pe.wait_ge(S["pt_out"], i0 + i - 2)
                        for j in range(n + 1):
                            ins = nc.tensor.transpose(ps[:, 4 + (i - 1) % 2, blk(j)], core_mem[:, S_P + (i - 1) % 2, blk(j)], const("ident"))
                        ins.then_inc(S["p_turned"], 1)
                    if i >= 2:
                        if i % 8 == 2 and i > 2:
                            outputs_turn()
                        n, c, hh = ITEMS[i - 2]
                        pe.wait_ge(S["pt_out"], i0 + i - 1)
                        at = HD * (2 * c + hh)
                        for j in range(n + 1):
                            ins = nc.tensor.matmul(ps[:, 6, at:at + HD], core_mem[:, S_PT + i % 2, blk(j)], mem[:, 45, j * P + HD * hh:j * P + HD * hh + HD],
                                                   start=(j == 0), stop=(j == n))
                        ins.then_inc(S["pv_done"], 1)
                outputs_turn()
                due("items", len(ITEMS))


            def outputs_turn():
                pe.wait_ge(S["o_taken"], due("o_taken"))
                if due("ot") > 1:
                    pe.wait_ge(S["y_att_out"], seen["ot"] - 1)
                for c in range(4):
                    ins = nc.tensor.transpose(ps[:, 7, blk(c)], core_mem[:, S_OUT, blk(c)], const("ident"))
                ins.then_inc(S["ot_ready"], 1)


            def turn(src, bank):
                for n in range(TB):
                    ins = nc.tensor.transpose(ps[:, bank, blk(n)], src[:, blk(n)], const("ident"))
                ins.then_inc(S["turned"], 1)


            def recurrences(l):
                pe.wait_ge(S["y_att_out"], 4 * (l + 1))
                if l > 0:
                    for c in range(2):
                        ins = nc.tensor.matmul(ps[0:32, 6, :], v_down[:, c, :], rw[:, 4 + c, 1:T + 1], start=(c == 0), stop=(c == 1))
                    ins.then_inc(S["vd_ready"], 1)
                    pe.wait_ge(S["vd_out"], 1)
                    for c in range(2):
                        ins = nc.tensor.matmul(ps[:, 7 - c, :], v_up[:, blk(c)], mem[0:32, 45, :], start=True, stop=True)
                    ins.then_inc(S["vu_ready"], 1)
                    pe.wait_ge(S["v_gate"], 1)
                normed = mem_units(39, 40, 41, 42)

                def turn_rwkv():
                    pe.wait_ge(S["rwkv_ready"], l + 1)
                    pe.wait_ge(S["bonus_taken"], l + 1)
                    for src in (mem[:, 7, :], mem[:, 8, :], rw[:, 2, 1:], rw[:, 3, 1:], rw[:, 4, 1:], rw[:, 5, 1:]):
                        n = due("turn")
                        if n > 2:
                            pe.wait_ge(S["turned_out"], n - 2)
                        turn(src, n % 2)

                if l == 0:
                    turn_rwkv()
                for pair in range(2):
                    pe.wait_ge(S["head_sq"], due("head_sq"))
                    ins = head_sums(normed[2 * pair:2 * pair + 2], 2, 2 * pair)
                ins.then_inc(S["head_sum"], 1)
                if l > 0:
                    turn_rwkv()
                pe.wait_ge(S["head_inv"], due("head_inv"))
                for c, chunk in enumerate(normed):
                    ins = head_spread(chunk, 2 + c)
                ins.then_inc(S["head_spread"], 1)
                pe.wait_ge(S["turned_out"], seen["turn"])
                pe.wait_ge(S["g_ready"], l + 1)
                pe.wait_ge(S["head_done"], due("head_done"))
                rows = slice(ROW_A, ROW_A + 4)
                for n in range(TB):
                    ins = nc.tensor.transpose(ps[:, 0, 4 * n:4 * n + 4], mem[rows, 6, blk(n)], const("ident", ROW_A, 4)[rows, :])
                ins.then_inc(S["g_turned"], 1)
                for c in range(2):
                    ins = nc.tensor.matmul(ps[:, 2 + c, :], const("sel_pair", c * P)[rows, :], mem[rows, 6, :], start=True, stop=True)
                ins.then_inc(S["spread_ready"], 1)
                pe.wait_ge(S["beta_ready"], l + 1)
                pe.wait_ge(S["g_taken"], l + 1)
                pe.wait_ge(S["bonus_taken"], l + 1)
                brows = slice(ROW_B, ROW_B + 4)
                for c in range(2):
                    ins = nc.tensor.matmul(ps[:, c, :], const("sel_pair", c * P)[brows, :], mem[brows, U_MISC, :], start=True, stop=True)
                ins.then_inc(S["spread_ready"], 1)
                for h in range(4):
                    nc.tensor.matmul(ps[:, 4 + h, :], const("sel_head", h * P)[rows, :], mem[rows, 6, :], start=True, stop=True).then_inc(S["spread_ready"], 1)
                pe.wait_ge(S["spread_taken"], 3 * l + 2)
                pe.wait_ge(S["kd_ready"], l + 1)
                for src in (mem[:, 37, :], mem[:, 38, :], mem[:, 24, :], mem[:, 25, :]):
                    n = due("turn")
                    pe.wait_ge(S["turned_out"], n - 2)
                    turn(src, n % 2)
                pe.wait_ge(S["turned_out"], seen["turn"])
                pe.wait_ge(S["gdn_ready"], l + 1)
                pe.wait_ge(S["eg_ready"], l + 1)
                pe.wait_ge(S["dt_ready"], l + 1)
                pe.wait_ge(S["spread_taken"], 3 * l + 3)
                for n in range(TB + 1):
                    core_step(l, n)
                post(l)


            def grams(banks, ready, pairs, n):
                for hh, bank in enumerate(banks):
                    rows = slice(HD * hh, HD * hh + HD)
                    for x, (left, right) in enumerate(pairs):
                        for c in range(2):
                            ins = nc.tensor.matmul(ps[:, bank, blk(2 * x + c)], left(c)[rows, blk(n)], right(c)[rows, blk(n)], start=True, stop=True)
                    ins.then_inc(S[ready], 1)


            def core_step(l, n):
                ap, nb = (lambda c: mem[:, 46 + c, :]), (lambda c: mem[:, 7 + c, :])
                rt, kt = (lambda c: rw[:, c, 1:T + 1]), (lambda c: rw[:, 2 + c, 1:T + 1])
                kg, kb, qg = (lambda c: mem[:, 35 + c, :]), (lambda c: mem[:, 39 + c, :]), (lambda c: mem[:, 33 + c, :])
                qe, kbe = (lambda c: mem[:, 37 + c, :]), (lambda c: mem[:, 24 + c, :])
                nb_t, kt_t, v_t, vb_t, kd_t = (0, 1), (4, 5), (2, 3), (26, 19), (45, 6)
                b = TB * l + n
                cm = core_mem
                last = n - 1
                tm = lambda u, hh: mem[:, u, last * P + HD * hh:last * P + HD * hh + HD]
                slot = lambda ru, hh, j: ru[:, 4 * HD * hh + HD * j:4 * HD * hh + HD * j + HD]

                def turned_products(lev, g):
                    e = 2 * (N_LEVELS * b + lev) + g
                    pe.wait_ge(S["n_ready"], e + 1)
                    if e >= 2:
                        pe.wait_ge(S["inv_ready"], e - 1)
                    for h in range(4):
                        right = const("ident") if lev == 0 else cm[:, C_INV + g, blk(h)]
                        ins = nc.tensor.matmul(ps[:, 2 + g, blk(h)], cm[:, C_N + g, blk(h)], right, start=True, stop=True)
                    ins.then_inc(S["t1_ready"], 1)

                def inverse_products(lev, g):
                    pe.wait_ge(S["t1_out"], 2 * ((N_LEVELS - 1) * b + lev - 1) + g + 1)
                    for h in range(4):
                        t1, inv_t = cm[:, C_T1 + g, blk(h)], cm[:, inv_t_unit(n, g), blk(h)]
                        out = lambda at: compact(ps[:, 4 + g, at + HD * h:at + HD * h + HD], lev)
                        if lev < N_LEVELS - 1:
                            nc.tensor.matmul(out(0), inv_t, evens(t1, lev), start=True, stop=True)
                        ins = nc.tensor.matmul(out(HALF), t1, odds(inv_t, lev), start=True, stop=True)
                    ins.then_inc(S["dx_ready"], 1)

                def a_grams():
                    if n < TB:
                        pe.wait_ge(S["gram_taken"], 2 * b + 2)
                    elif n > 1:
                        pe.wait_ge(S["s_out"], b)
                    if b > 1:
                        pe.wait_ge(S["y_out"], b - 1)
                    grams((0, 1), "a_gram_ready", ((kt, ap), (kt, rt)), last)
                    grams((6, 7), "a_gram_ready", ((nb, rt), (kg, qg)), last)

                def right_sides():
                    pe.wait_ge(S["inv_ready"], 2 * N_LEVELS * b)
                    pe.wait_ge(S["a_gram_out"], 4 * b)
                    pe.wait_ge(S["s_out"], b)
                    for hh in range(2):
                        rows = slice(HD * hh, HD * hh + HD)
                        for j in range(4):
                            c = j % 2
                            out_r = ps[:, 6 + hh, HD * j:HD * j + HD]
                            left = ap(c) if j < 2 else kbe(c)
                            nc.tensor.matmul(out_r, left[rows, blk(last)], state[rows, j, :], start=True, stop=False)
                            if j < 2:
                                ins = nc.tensor.matmul(out_r, cm[:, C_A + hh, blk(c)], tm(v_t[c], hh), start=False, stop=True)
                            else:
                                ins = nc.tensor.matmul(out_r, const("ident"), tm(vb_t[c], hh), start=False, stop=True)
                    ins.then_inc(S["r_ready"], 1)

                def writes():
                    pe.wait_ge(S["r_out"], b)
                    for hh in range(2):
                        for j in range(4):
                            at = 4 * HD * hh + HD * j
                            ins = nc.tensor.matmul(ps[:, 0, at:at + HD], cm[:, inv_t_unit(last, hh), blk(j)], slot(C_R, hh, j), start=True, stop=True)
                    ins.then_inc(S["u_ready"], 1)

                def outputs():
                    pe.wait_ge(S["u_out"], b)
                    if n < TB:
                        for hh in range(2):
                            for j in range(4):
                                c = j % 2
                                out_s = ps[HD * hh:HD * hh + HD, 1, HD * j:HD * j + HD]
                                if j < 2:
                                    nc.tensor.matmul(out_s, tm(nb_t[c], hh), slot(C_U, hh, j), start=True, stop=False)
                                    ins = nc.tensor.matmul(out_s, tm(kt_t[c], hh), tm(v_t[c], hh), start=False, stop=True)
                                else:
                                    ins = nc.tensor.matmul(out_s, tm(kd_t[c], hh), slot(C_U, hh, j), start=True, stop=True)
                        ins.then_inc(S["s_next"], 1)
                    for hh in range(2):
                        rows = slice(HD * hh, HD * hh + HD)
                        for j in range(4):
                            c = j % 2
                            out_y = ps[rows, 6, blk(j)]
                            q = rt(c) if j < 2 else qe(c)
                            nc.tensor.matmul(out_y, state[rows, j, :], q[rows, blk(last)], start=True, stop=False)
                            if j < 2:
                                nc.tensor.matmul(out_y, tm(v_t[c], hh), cm[:, C_A + hh, blk(2 + c)], start=False, stop=False)
                            ins = nc.tensor.matmul(out_y, slot(C_U, hh, j), cm[:, C_A + 2 + hh, blk(j)], start=False, stop=True)
                    ins.then_inc(S["y_ready"], 1)

                if n < TB:
                    if n > 1:
                        pe.wait_ge(S["s_out"], b)
                    grams((0, 1), "gram_ready", ((nb, ap), (kg, kb)), n)
                for lev in range(N_LEVELS):
                    if n < TB:
                        for g in range(2):
                            turned_products(lev, g)
                    stage = {0: a_grams, 2: right_sides, 3: writes, 5: outputs}.get(lev)
                    if n and stage:
                        stage()
                    if n < TB and lev:
                        for g in range(2):
                            inverse_products(lev, g)


            def post(l):
                pe.wait_ge(S["y_out"], TB * (l + 1))
                for c in range(2):
                    ins = nc.tensor.matmul(ps[:, c, :], const("ones_head"), rw[:, c, 1:T + 1], start=True, stop=True)
                ins.then_inc(S["mean_ready"], 1)
                head_norms(mem_units(35, 36), 4, (4, 5))
                head_norms(mem_units(33, 34), 2, (2, 3))
                due("head_done", 2)
                base = BASE[f"mix_out{l}"]
                out_tiles(base)


            def out_tiles(base, order=range(KD)):
                first_tiles(base, (7, 0), order)
                for k in range(2, KD):
                    linear_tile(ps[:, k - 1, :], base + k)
                    if k >= 3:
                        sum_chunk(k - 3)


            def linear_ctx(bank, t):
                for k in range(KD):
                    products(bank, t % RING, k * P, hc_hi[:, k, :], hc_lo[:, k, :], k == 0, k == KD - 1)


            def mla():
                base = BASE["mla_in"]
                first = seen["proj_out"]
                sum_squares()
                first_tiles(base)
                pe.wait_ge(S["ctx_sq"], 1)
                for k in range(KD):
                    ins = nc.tensor.matmul(ps[:, 6, 0:CTX], const("ones"), ctx_sq[:, k, :], start=(k == 0), stop=(k == KD - 1))
                ins.then_inc(S["ctx_sum"], 1)
                for m in range(2, 6):
                    pe.wait_ge(S["proj_out"], first + m - 1)
                    if m >= 3:
                        pe.wait_ge(S["ctx_ready"], 1)
                        pe.wait_ge(S["w_lo_ready"], base + m + 1)
                        if m == 5:
                            pe.wait_ge(S["ctx_out"], 1)
                        linear_ctx(ps[:, 2 + m % 2, 0:CTX], base + m)
                    linear_tile(ps[:, m % 2, :], base + m)
                pe.wait_ge(S["proj_out"], first + 6)
                pe.wait_ge(S["ctx_out"], 3)
                for j in range(4):
                    if j:
                        pe.wait_ge(S["c_out"], j)
                    linear_tile(ps[:, 0, :], base + 6 + 3 * j)
                    if j == 0:
                        pe.wait_ge(S["lat_sq"], 2)
                        lat_squares = [mem2[:, CQ_STD + c, :] for c in range(3)], [ckv_sq[:, c, :] for c in range(2)]
                        for which, chunks in enumerate(lat_squares):
                            for n in range((TB, KB)[which]):
                                at = TB * which + n
                                for c, chunk in enumerate(chunks):
                                    ins = nc.tensor.matmul(ps[:, 4, at:at + 1], chunk[:, blk(n)], const("ones", 0, 1), start=(c == 0), stop=(c == len(chunks) - 1))
                        ins.then_inc(S["lat_sum"], 1)
                    if j:
                        pe.wait_ge(S["u_taken"], j)
                    linear_tile(ps[:, 1, :], base + 7 + 3 * j)
                    if j:
                        pe.wait_ge(S["conv_taken"], j)
                    linear_tile(ps[:, 2, :], base + 8 + 3 * j)
                    if j == 0:
                        pe.wait_ge(S["lat_inv"], 1)
                        pe.wait_ge(S["ctx_std"], 1)
                        for at in range(TB + KB):
                            ins = nc.tensor.matmul(psf[:, 4 * T + at * P:4 * T + (at + 1) * P], head_tok[:, at:at + 1].to_broadcast([P, P]), const("ident"), start=True, stop=True)
                        ins.then_inc(S["lat_spread"], 1)
                pe.wait_ge(S["lat_ready"], 2)
                pe.wait_ge(S["conv_taken"], 4)

                def qk_sum(i):
                    pe.wait_ge(S["qk_sq"], i + 1)
                    if i:
                        pe.wait_ge(S["qk_std"], i)
                    for n in range(qk_width(i) // P):
                        ins = nc.tensor.matmul(ps[:, 6, n:n + 1], wide[i % 2][0:QKD, blk(n)], const("ones", 0, 1)[0:QKD, :], start=True, stop=True)
                    ins.then_inc(S["qk_sum"], 1)

                def qk_spread(i):
                    pe.wait_ge(S["qk_inv"], i + 1)
                    if i:
                        pe.wait_ge(S["qk_done"], i)
                    for n in range(qk_width(i) // P):
                        at = 4 * T + n * P
                        ins = nc.tensor.matmul(psf[0:QKD, at:at + P], qk_tok(i)[:, n:n + 1].to_broadcast([P, QKD]), const("ident"), start=True, stop=True)
                    ins.then_inc(S["qk_spread"], 1)

                def qk_rotate(i):
                    pe.wait_ge(S["qk_done"], i + 1)
                    pe.wait_ge(S["consts2_loaded"], 16)
                    if i:
                        pe.wait_ge(S["rot2_done"], i)
                    src = mem2[PE_ROWS, Q_MLA + i, :] if i < 8 else kmla[PE_ROWS, i - 8, 0:T]
                    nc.tensor.matmul(ps[PE_ROWS, 7, :], const2("rot2", P)[PE_ROWS, PE_ROWS], src, start=True, stop=True).then_inc(S["rot2_ready"], 1)

                def qk_steps(i):
                    for step, late in ((qk_sum, 1), (qk_spread, 2), (qk_rotate, 3)):
                        if 0 <= i - late < 16:
                            step(i - late)

                base = BASE["mla_q"]
                for h in range(8):
                    t = base + h // 2
                    pe.wait_ge(S["w_lo_ready"], t + 1)
                    if h >= 2:
                        pe.wait_ge(S["qk_out"], h - 1)
                    for k in range(3):
                        ins = products(ps[:, 2 * (h % 2), :], t % RING, (3 * (h % 2) + k) * P, cq_hi[:, k, :], cq_lo[:, k, :], k == 0, k == 2)
                    ins.then_inc(S["w_used"] if h % 2 else S["qk_ready"], 1)
                    qk_steps(h)
                base = BASE["mla_kv"]
                for h in range(8):
                    t = base + h // 4
                    pe.wait_ge(S["w_lo_ready"], t + 1)
                    pe.wait_ge(S["qk_out"], 8 + max(h - 1, 0))
                    for k in range(2):
                        products(ps[:, 2 * (h % 2), :], t % RING, (2 * (h % 4) + k) * P, ckv_hi[:, k, 0:T], ckv_lo[:, k, 0:T], k == 0, k == 1)
                    for k in range(2):
                        ins = products(ps[:, 2 * (h % 2) + 1, 0:CTX], t % RING, (2 * (h % 4) + k) * P, ckv_hi[:, k, T:TK], ckv_lo[:, k, T:TK], k == 0, k == 1)
                    ins.then_inc(S["w_used"] if h % 4 == 3 else S["qk_ready"], 1)
                    qk_steps(8 + h)
                for i in range(16, 19):
                    qk_steps(i)
                t = base + 2
                pe.wait_ge(S["w_lo_ready"], t + 1)
                pe.wait_ge(S["qk_out"], 16)
                for n in range(6):
                    if n >= 4:
                        pe.wait_ge(S["vtok_out"], n - 3)
                    for k in range(2):
                        wh, wl = (w[:, t % RING, k * T:(k + 1) * T] for w in (w_hi, w_lo))
                        lh, ll = (a[:, k, blk(n)] for a in (ckv_hi, ckv_lo))
                        nc.tensor.matmul(ps[:, n % 4, :], lh, wh, start=(k == 0), stop=False)
                        nc.tensor.matmul(ps[:, n % 4, :], lh, wl, start=False, stop=False)
                        ins = nc.tensor.matmul(ps[:, n % 4, :], ll, wh, start=False, stop=(k == 1))
                    ins.then_inc(S["w_used"] if n == 5 else S["vtok_ready"], 1)
                pe.wait_ge(S["rot2_done"], 16)
                pe.wait_ge(S["vtok_out"], 6)
                items = [(n, h) for n in range(TB) for h in range(8)]
                i0, t0 = seen["items"], seen["ot"]
                for i in range(len(items) + 2):
                    if i < len(items):
                        n, h = items[i]
                        if i >= 2:
                            pe.wait_ge(S["p_ready"], i0 + i - 1)
                        q = mem2[0:QKD, Q_MLA + h, blk(n)]
                        nc.tensor.matmul(ps[:, 2 * (i % 2), :], q, kmla[0:QKD, h, 0:T], start=True, stop=True)
                        nc.tensor.matmul(ps[:, 2 * (i % 2) + 1, 0:CTX], q, kmla[0:QKD, h, T:TK], start=True, stop=True).then_inc(S["s_ready"], 1)
                    if 1 <= i <= len(items):
                        pe.wait_ge(S["p_ready"], i0 + i)
                        if i >= 2:
                            pe.wait_ge(S["pt_out"], i0 + i - 1)
                        for j in range(6):
                            ins = nc.tensor.transpose(psf[:, 4 * T + j * P:4 * T + (j + 1) * P], probs[(i - 1) % 2][:, blk(j)], const("ident"))
                        ins.then_inc(S["p_turned"], 1)
                    if i >= 2:
                        if i % 8 == 2 and i > 2:
                            mla_outputs_turn()
                        h = items[i - 2][1]
                        pe.wait_ge(S["pt_out"], i0 + i - 1)
                        for j in range(6):
                            ins = nc.tensor.matmul(ps[:, 6, HD * h:HD * h + HD], wide[i % 2][:, blk(j)], vtok[:, j, HD * h:HD * h + HD], start=(j == 0), stop=(j == 5))
                        ins.then_inc(S["pv_done"], 1)
                mla_outputs_turn()
                due("items", len(items))
                out_tiles(BASE["mla_out"])


            def mla_outputs_turn():
                pe.wait_ge(S["o_taken"], due("o_taken"))
                pe.wait_ge(S["y_att_out"], due("ot") - 1)
                for c in range(4):
                    ins = nc.tensor.transpose(ps[:, 7, blk(c)], mem2[:, O_MLA, blk(c)], const("ident"))
                ins.then_inc(S["ot_ready"], 1)


            def fourier():
                sum_squares()
                t = BASE["dft_group"]
                pe.wait_ge(S["w_lo_ready"], t + 1)
                for i in range(16):
                    g, n = i // 4, i % 4
                    if n == 0:
                        pe.wait_ge(S["h_ready"], due("h_ready", 2))
                    if i >= 4:
                        pe.wait_ge(S["g_split"], i - 3)
                    for k in range(2):
                        wh, wl = (w[:, t % RING, k * T:(k + 1) * T] for w in (w_hi, w_lo))
                        lh, ll = (a[:, 2 * g + k, blk(n)] for a in (h_hi, h_lo))
                        nc.tensor.matmul(ps[:, i % 4, :], lh, wh, start=(k == 0), stop=False)
                        nc.tensor.matmul(ps[:, i % 4, :], lh, wl, start=False, stop=False)
                        ins = nc.tensor.matmul(ps[:, i % 4, :], ll, wh, start=False, stop=(k == 1))
                    ins.then_inc(S["w_used"] if i == 15 else S["g_done"], 1)
                pe.wait_ge(S["g_split"], 16)
                for m in range(4):
                    t = BASE["dft_time"] + m
                    pe.wait_ge(S["w_lo_ready"], t + 1)
                    for tc in range(2):
                        n = 2 * (m % 2) + tc
                        wh, wl = (w[:, t % RING, tc * T:(tc + 1) * T] for w in (w_hi, w_lo))
                        for c in range(KD):
                            at = slice((m // 2) * 2 * P + (c % 2) * P, (m // 2) * 2 * P + (c % 2) * P + P)
                            lh, ll = (a[:, 4 * (c // 2) + n, at] for a in (g_hi, g_lo))
                            start, stop = m == 0 and tc == 0, m == 3 and tc == 1
                            nc.tensor.matmul(ps[:, c, :], lh, wh, start=start, stop=False, skip_group_check=True)
                            nc.tensor.matmul(ps[:, c, :], lh, wl, start=False, stop=False, skip_group_check=True)
                            ins = nc.tensor.matmul(ps[:, c, :], ll, wh, start=False, stop=stop, skip_group_check=True)
                    ins.then_inc(S["w_used"], 1)
                pe.wait_ge(S["h_ready"], seen["h_ready"] + 2)
                out_tiles(BASE["fourier_out"], FROM_LAST)
            for name in run:
                l = int(name[-1]) if name[-1].isdigit() else None
                if name.startswith("ffn"):
                    ffn(l)
                if name == "ffn0":
                    pe.wait_ge(S["consts_loaded"], 64)
                if name.startswith("rec_in"):
                    attention(l)
                if name.startswith("mix_out"):
                    recurrences(l)
                if name == "mla_out":
                    mla()
                if name == "fourier_out":
                    fourier()


def _tiles(w):
    k, m = w.shape
    return w.reshape(k // P, P, m // P, P).transpose(2, 1, 0, 3).reshape(m // P, P, k)


def _pad(w, width):
    return np.concatenate([w, np.zeros(w.shape[:-1] + (width - w.shape[-1],), w.dtype)], -1)


def _ffn_tiles(gate, up, down):
    g, u = _tiles(gate), _tiles(up)
    both = np.stack([g, u], 1).reshape(2 * NF, P, TILE)
    d = down.reshape(NF // 2, 2, P, 2, 4 * P).transpose(3, 0, 2, 1, 4)[::-1].reshape(NF, P, TILE)
    return [both, d]


def _mix_in_columns():
    zero = [3280]
    run = lambda at, n: list(range(at, at + n))
    q, k, v, qi, ki, wi = 0, 512, 640, 768, 1280, 1344
    rwkv, gdn = 1352, 2248
    misc = zero * P
    misc[ROW_WI:ROW_WI + 8] = run(wi, 8)
    misc[ROW_B:ROW_B + 4] = run(gdn + 1024, 4)
    misc[ROW_A:ROW_A + 4] = run(gdn + 1028, 4)
    cols = run(ki, HD) + run(ki, HD) + misc + run(qi, 512) + run(k, P)
    for c in range(4):
        cols += run(q + HD * c, HD) + run(q + HD * (c + 4), HD)
    return cols + run(v, P) + run(rwkv, 896) + run(gdn, 1024)


def _tile_stream(a):
    zeros = np.zeros((D, 1), np.float32)
    out = []
    for layer in range(DEPTH):
        out += _ffn_tiles(a["ffn_w_gate"][layer, 0], a["ffn_w_up"][layer, 0], a["ffn_w_down"][layer, 0])
        out.append(_tiles(np.concatenate([a["w_in"][layer], zeros], 1)[:, _mix_in_columns()]))
        rows = [HD * h + i for c in range(4) for h in (c, c + 4) for i in range(HD)] + list(range(512, D))
        out.append(_tiles(a["w_out"][layer][rows]))
        out += _ffn_tiles(a["ffn_w_gate"][layer, 1], a["ffn_w_up"][layer, 1], a["ffn_w_down"][layer, 1])
    w = np.concatenate([a["w_in_2"][0], zeros], 1)
    run = lambda at, n: list(range(at, at + n))
    cols = run(0, 640) + [2208] * HD + run(640, 32) + [2208] * 32
    for j in range(4):
        for part in (1, 2, 0):
            cols += run(672 + 512 * part + P * j, P)
    out.append(_tiles(w[:, cols]))
    uq = _pad(a["w_uq_2"][0].reshape(3, P, 8, QKD), P)
    out.append(_pad(uq.transpose(2, 1, 0, 3).reshape(4, 2, P, 3 * P).transpose(0, 2, 1, 3).reshape(4, P, 6 * P), TILE))
    ukv = a["w_ukv_2"][0].reshape(2, P, 8, 2, HD)
    uk = _pad(ukv[:, :, :, 0], P)
    out.append(uk.transpose(2, 1, 0, 3).reshape(2, 4, P, 2 * P).transpose(0, 2, 1, 3).reshape(2, P, TILE))
    out.append(ukv[:, :, :, 1].transpose(1, 0, 2, 3).reshape(1, P, TILE))
    out.append(_tiles(a["w_o_2"][0]))
    out += _ffn_tiles(a["ffn_w1_2"][0], a["ffn_w3_2"][0], a["ffn_w2_2"][0])
    g = 2 * np.pi * np.outer(np.arange(256), np.arange(256)) / 256
    dft_g = np.concatenate([np.cos(g), np.sin(g)], 1).astype(np.float32)
    out.append(dft_g.reshape(2, P, 512).transpose(1, 0, 2).reshape(1, P, TILE))
    t = 2 * np.pi * (np.outer(np.arange(T), np.arange(T)) % T) / T
    for m in (np.cos(t), -np.sin(t)):
        m = (m / np.sqrt(T * 256)).astype(np.float32)
        out.append(m.reshape(2, 2, P, T).transpose(0, 2, 1, 3).reshape(2, P, TILE))
    out.append(_tiles(a["w_fourier_2"][0]))
    out += _ffn_tiles(a["ffn_w1_2"][1], a["ffn_w3_2"][1], a["ffn_w2_2"][1])
    out = np.concatenate(out, 0)
    assert out.shape == (N_TILES, P, TILE)
    return out


def _params(a):
    out = np.zeros((P, N_PARAMS), np.float32)

    def put(name, v, rows=slice(0, P)):
        v = np.asarray(v).reshape(-1, rows.stop - rows.start).T
        out[rows, PARAM_AT[name]:PARAM_AT[name] + v.shape[1]] = v

    put("ffn_g", np.concatenate([a["ffn_norm"].reshape(4, D), a["norm2_g_2"]]))
    put("mix_g", np.concatenate([a["mix_norm"], a["norm1_g_2"]]))
    put("ada_b", a["ada_b_2"])
    rows = slice(ROW_A, ROW_A + 4)
    for n in range(DEPTH):
        put(f"mu{n}", a["rwkv_mu"][n])
        for name in ("w0", "a0", "k_k", "k_a", "r_k", "gn_w", "gn_b"):
            put(f"{name}{n}", a["rwkv_" + name][n])
        put(f"conv{n}", a["gdn_conv"][n])
        put(f"o_norm{n}", np.tile(a["gdn_o_norm"][n], 2))
        put(f"a_log{n}", a["gdn_a_log"][n], rows)
        put(f"dt{n}", a["gdn_dt_bias"][n], rows)
        put(f"att_q{n}", np.tile(a["att_q_norm"][n], 2))
        put(f"att_k{n}", np.tile(a["att_k_norm"][n], 2))
    put("v0", a["rwkv_v0"][0])
    put("mla_qn", a["q_norm_g_2"][0])
    put("mla_kvn", a["kv_norm_g_2"][0])
    put("q_gain", a["q_gain_2"][0], slice(0, QKD))
    put("k_gain", a["k_gain_2"][0], slice(0, QKD))
    put("short_conv", a["conv_w_2"][0])
    return out


def _consts():
    f32 = np.float32
    p, q = np.arange(P)[:, None], np.arange(P)[None, :]
    c = {"ident": p == q, "ones": np.ones((P, P)), "ones_head": p // HD == q // HD}
    half = HD // 2
    c["rot"] = (q % HD < half) * (p == q + half) * -1.0 + (q % HD >= half) * (p == q - half) * 1.0
    inv = f32(10000.0) ** (-np.arange(half, dtype=f32) / f32(half))
    ang = inv.astype(f32)[np.arange(P) % half][:, None] * np.arange(T, dtype=f32)[None, :]
    c["cos"], c["sin"] = np.cos(ang), np.sin(ang)
    c["strict"], c["incl"] = p < q, p <= q
    c["causal_neg"] = np.where(q <= p, 0.0, NEG)
    c["decay_neg"] = np.where(p <= q, 0.0, NEG)
    m = [1 << n for n in range(N_LEVELS)]
    c["levels"] = np.concatenate([((q // s) % 2 == 1) & (p // s == q // s - 1) for s in m], 1)
    row = np.where((p >= ROW_B) & (p < ROW_B + 4), p - ROW_B, np.where((p >= ROW_A) & (p < ROW_A + 4), p - ROW_A, -1))
    c["sel_pair"] = np.concatenate([row == 2 * n + q // HD for n in range(2)], 1)
    c["sel_head"] = np.concatenate([(row == h) & (q >= 0) for h in range(4)], 1)
    c["eps"] = np.tile(np.array([[NORM_EPS, L2_EPS, GN_EPS, 1.0]]), (P, 1))
    first = np.concatenate([np.asarray(c[n], f32) for n, _ in CONSTS], 1)
    pe = p - HD
    in_pe = (p >= HD) & (p < QKD)
    rot2 = np.zeros((P, P))
    for i in range(32):
        rot2[HD + (i + 8 if i % 16 < 8 else i - 8), HD + i] = -1.0 if i % 16 < 8 else 1.0
    t = np.arange(T)[None, :]
    inv2 = f32(1.0) / (f32(10000.0) ** (np.arange(0, 16, 2, dtype=f32) / f32(16)))
    ang2 = np.where(pe % 32 < 16, t // 64, t % 64).astype(f32) * inv2[pe % 8]
    c2 = {"rot2": rot2, "cos2": np.where(in_pe, np.cos(ang2), 1.0), "sin2": np.where(in_pe, np.sin(ang2), 0.0)}
    second = np.concatenate([np.asarray(c2[n], f32) for n, _ in CONSTS_2], 1)
    return first, second


def kernel(**inputs):
    import concourse.bacc as bacc
    from concourse.bass_utils import run_bass_kernel_spmd

    a = {n: np.asarray(v) for n, v in inputs.items()}
    consts, consts_2 = _consts()
    arrays = {
        "x_t": np.ascontiguousarray(a["x"][0].T),
        "ctx_t": np.ascontiguousarray(a["ctx_2"][0].T),
        "tiles": _tile_stream(a),
        "ada_tiles": np.ascontiguousarray(a["ada_w_2"].transpose(0, 2, 1)).reshape(ADA_TILES, P, D),
        "cond": np.stack([a["c_2"].reshape(D), a["c_ctx_2"].reshape(D)]),
        "params": _params(a),
        "consts": consts,
        "consts_2": consts_2,
        "lora": np.concatenate([a["rwkv_w_up"], a["rwkv_a_up"], a["rwkv_g_up"]], 1),
        "v_down": np.ascontiguousarray(a["rwkv_v_down"][0]),
        "v_up": np.ascontiguousarray(a["rwkv_v_up"][0]),
    }
    nc = bacc.Bacc("TRN2", target_bir_lowering=False, num_devices=1)
    io = {n: nc.dram_tensor("in_" + n, v.shape, mybir.dt.from_np(v.dtype), kind="ExternalInput").ap() for n, v in arrays.items()}
    out = nc.dram_tensor("out_t", (D, T), F32, kind="ExternalOutput").ap()
    build_program(nc, io, out)
    r = run_bass_kernel_spmd(nc, [{"in_" + n: v for n, v in arrays.items()}], core_ids=[0])
    return np.ascontiguousarray(r.results[0]["out_t"].T)[None]
```
